# Optimizing a Trainium2 kernel written in Bass

```python
import jax, jax.numpy as jnp
from jax import lax
import numpy as np

D_MODEL = 1024
BATCH = 1
SEQ = 512
DEPTH = 2

N_EVEN = (DEPTH + 1) // 2
N_ODD = DEPTH // 2
EPS = 1e-6

D_FF = 2816

N_MEM = 256
XA_HEADS = 4
XA_HEAD_DIM = D_MODEL // XA_HEADS

A_HEADS = 8
A_HEAD_DIM = 64
A_WIDTH = A_HEADS * A_HEAD_DIM
KV_RANK = 256
IDX_HEADS = 8
IDX_DIM = 64
TOPK_MAX = 256
Q_BLOCK = 128
B_WIDTH = D_MODEL - A_WIDTH
B_BLOCKS = 8
B_BLOCK_DIM = B_WIDTH // B_BLOCKS
CONV_W = 4
LRU_C = 8.0
EVEN_SPLITS = (A_WIDTH, KV_RANK, IDX_HEADS * IDX_DIM, IDX_DIM, IDX_HEADS, B_WIDTH, B_WIDTH)
EVEN_IN = sum(EVEN_SPLITS)

GLA_HEADS = 4
GLA_DK = D_MODEL // 2
GLA_DV = D_MODEL
GLA_DKH = GLA_DK // GLA_HEADS
GLA_DVH = GLA_DV // GLA_HEADS
GLA_GATE_RANK = 16
GLA_TAU = 16.0
GLA_CHUNK = 64
ODD_SPLITS = (GLA_DK, GLA_DK, GLA_DV, GLA_GATE_RANK, GLA_DV)
ODD_IN = sum(ODD_SPLITS)

N_FFN1_PRE, N_FFN1_POST, N_MIX_PRE, N_MIX_POST, N_XA_PRE, N_XA_POST, N_MEM_NORM, N_FFN2_PRE, N_FFN2_POST = range(9)
N_NORMS = 9

kernel_name = "hybrid_dsa_rglru_gla_macaron_block"

def _split(t, sizes):
    return jnp.split(t, np.cumsum(sizes)[:-1].tolist(), axis=-1)

def rmsnorm(x, g):
    xf = x.astype(jnp.float32)
    y = xf * lax.rsqrt(jnp.mean(xf * xf, axis=-1, keepdims=True) + EPS)
    return (y * g.astype(jnp.float32)).astype(x.dtype)

def swiglu(x, w_gu, w_down):
    g, u = jnp.split(x @ w_gu, 2, axis=-1)
    return (jax.nn.silu(g) * u) @ w_down

def causal_dwconv(x, w, b):
    y = lax.conv_general_dilated(x, w[:, None, :].astype(x.dtype), window_strides=(1,),
                                 padding=[(CONV_W - 1, 0)], dimension_numbers=('NWC', 'WIO', 'NWC'),
                                 feature_group_count=x.shape[-1])
    return y + b

def rg_lru(xc, w_ra, b_ra, w_ri, b_ri, lam):
    Bb, S, _ = xc.shape
    xb = xc.reshape(Bb, S, B_BLOCKS, B_BLOCK_DIM)
    r = jax.nn.sigmoid((jnp.einsum('bsgi,gij->bsgj', xb, w_ra) + b_ra).astype(jnp.float32)).reshape(Bb, S, B_WIDTH)
    i = jax.nn.sigmoid((jnp.einsum('bsgi,gij->bsgj', xb, w_ri) + b_ri).astype(jnp.float32)).reshape(Bb, S, B_WIDTH)
    log_a = -LRU_C * r * jax.nn.softplus(-lam.astype(jnp.float32))
    a = jnp.exp(log_a)
    b = jnp.sqrt(-jnp.expm1(2.0 * log_a)) * (i * xc.astype(jnp.float32))

    def combine(left, right):
        a1, b1 = left
        a2, b2 = right
        return a1 * a2, a2 * b1 + b2

    _, h = lax.associative_scan(combine, (a, b), axis=1)
    return h.astype(xc.dtype)

def dsa_attention(q, k, v, q_idx, k_idx, w_idx):
    Bb, S = q.shape[0], q.shape[1]
    n_blk = S // Q_BLOCK
    top_k = min(TOPK_MAX, S // 4)
    key_pos = jnp.arange(S)

    def block(args):
        qb, qib, wb, start = args
        t = start + jnp.arange(Q_BLOCK)
        sc = jnp.einsum('bqhd,bsd->bqhs', qib, k_idx, preferred_element_type=jnp.float32) * (IDX_DIM ** -0.5)
        score = jnp.einsum('bqhs,bqh->bqs', jax.nn.relu(sc), wb.astype(jnp.float32) * (IDX_HEADS ** -0.5))
        causal = key_pos[None, :] <= t[:, None]
        score = jnp.where(causal[None], score, -jnp.inf)
        _, idx = lax.top_k(score, top_k)
        kg = jax.vmap(lambda kk, ii: kk[ii])(k, idx)
        vg = jax.vmap(lambda vv, ii: vv[ii])(v, idx)
        s = jnp.einsum('bqhd,bqkhd->bqhk', qb, kg, preferred_element_type=jnp.float32) * (A_HEAD_DIM ** -0.5)
        valid = (idx <= t[None, :, None])[:, :, None, :]
        p = jax.nn.softmax(jnp.where(valid, s, -jnp.inf), axis=-1)
        return jnp.einsum('bqhk,bqkhd->bqhd', p.astype(vg.dtype), vg)

    def to_blocks(a):
        return a.reshape(Bb, n_blk, Q_BLOCK, *a.shape[2:]).swapaxes(0, 1)

    starts = jnp.arange(n_blk) * Q_BLOCK
    out = lax.map(block, (to_blocks(q), to_blocks(q_idx), to_blocks(w_idx), starts))
    return out.swapaxes(0, 1).reshape(q.shape)

def even_mixer(h, w_in, kv_norm, w_uk, w_uv, conv_w, conv_b, w_ra, b_ra, w_ri, b_ri, lam, w_out):
    Bb, S, _ = h.shape
    q, c_kv, q_i, k_i, w_i, gate_b, x_b = _split(h @ w_in, EVEN_SPLITS)
    c_kv = rmsnorm(c_kv, kv_norm)
    k = (c_kv @ w_uk).reshape(Bb, S, A_HEADS, A_HEAD_DIM)
    v = (c_kv @ w_uv).reshape(Bb, S, A_HEADS, A_HEAD_DIM)
    a_out = dsa_attention(q.reshape(Bb, S, A_HEADS, A_HEAD_DIM), k, v,
                          q_i.reshape(Bb, S, IDX_HEADS, IDX_DIM), k_i, w_i).reshape(Bb, S, A_WIDTH)
    xc = causal_dwconv(x_b, conv_w, conv_b)
    b_out = rg_lru(xc, w_ra, b_ra, w_ri, b_ri, lam) * jax.nn.gelu(gate_b)
    return jnp.concatenate([a_out, b_out], axis=-1) @ w_out

def gla_mixer(h, w_in, w_g2, b_g, head_norm, w_out):
    Bb, S, _ = h.shape
    nc = S // GLA_CHUNK
    q, k, v, g_lr, r = _split(h @ w_in, ODD_SPLITS)
    gk = jax.nn.log_sigmoid((g_lr @ w_g2 + b_g).astype(jnp.float32)) / GLA_TAU

    def chunks(a, dh):
        return a.astype(jnp.float32).reshape(Bb, nc, GLA_CHUNK, GLA_HEADS, dh).transpose(0, 1, 3, 2, 4)

    q = chunks(q, GLA_DKH) * (GLA_DKH ** -0.5)
    k = chunks(k, GLA_DKH)
    v = chunks(v, GLA_DVH)
    G = jnp.cumsum(chunks(gk, GLA_DKH), axis=3)
    G_last = G[:, :, :, -1:, :]
    q_dec = q * jnp.exp(G)
    k_inv = k * jnp.exp(-G)
    k_rem = k * jnp.exp(G_last - G)
    tril = jnp.tril(jnp.ones((GLA_CHUNK, GLA_CHUNK), dtype=bool))
    att = jnp.where(tril, jnp.einsum('bnhid,bnhjd->bnhij', q_dec, k_inv), 0.0)
    o_intra = jnp.einsum('bnhij,bnhjv->bnhiv', att, v)

    def step(state, xs):
        qd, kr, vv, dec = xs
        o = jnp.einsum('bhid,bhdv->bhiv', qd, state)
        state = dec[..., None] * state + jnp.einsum('bhjd,bhjv->bhdv', kr, vv)
        return state, o

    s0 = jnp.zeros((Bb, GLA_HEADS, GLA_DKH, GLA_DVH), jnp.float32)
    xs = (q_dec.swapaxes(0, 1), k_rem.swapaxes(0, 1), v.swapaxes(0, 1), jnp.exp(G_last[:, :, :, 0, :]).swapaxes(0, 1))
    _, o_inter = lax.scan(step, s0, xs)
    o = o_intra + o_inter.swapaxes(0, 1)
    o = o.transpose(0, 1, 3, 2, 4).reshape(Bb, S, GLA_HEADS, GLA_DVH)
    o = rmsnorm(o, head_norm).reshape(Bb, S, GLA_DV).astype(h.dtype) * jax.nn.silu(r)
    return o @ w_out

def mem_cross_attention(h, mem_n, w_q, w_kv, w_o):
    Bb, S, _ = h.shape
    M = mem_n.shape[1]
    q = (h @ w_q).reshape(Bb, S, XA_HEADS, XA_HEAD_DIM)
    k, v = jnp.split(mem_n @ w_kv, 2, axis=-1)
    k = k.reshape(Bb, M, XA_HEADS, XA_HEAD_DIM)
    v = v.reshape(Bb, M, XA_HEADS, XA_HEAD_DIM)
    s = jnp.einsum('bshd,bmhd->bhsm', q, k, preferred_element_type=jnp.float32) * (XA_HEAD_DIM ** -0.5)
    p = jax.nn.softmax(s, axis=-1)
    o = jnp.einsum('bhsm,bmhd->bshd', p.astype(v.dtype), v).reshape(Bb, S, D_MODEL)
    return o @ w_o

def setup_inputs(seed: int = 0) -> dict:
    key = jax.random.key(seed)
    ks = iter(jax.random.split(key, 32))
    f32 = jnp.float32

    def nrm(shape, fan_in):
        return jax.random.normal(next(ks), shape, f32) * (fan_in ** -0.5)

    def small(shape, scale=0.01):
        return jax.random.normal(next(ks), shape, f32) * scale

    def gain(shape):
        return 1.0 + jax.random.normal(next(ks), shape, f32) * 0.02

    u = jax.random.uniform(next(ks), (N_EVEN, B_WIDTH), f32, 0.9, 0.999)
    a_base = u ** (1.0 / LRU_C)
    lam = jnp.log(a_base) - jnp.log1p(-a_base)

    return {
        "x": jax.random.normal(next(ks), (BATCH, SEQ, D_MODEL), f32),
        "mem": jax.random.normal(next(ks), (BATCH, N_MEM, D_MODEL), f32),
        "norms": gain((DEPTH, N_NORMS, D_MODEL)),
        "ffn_w_gu": nrm((DEPTH, 2, D_MODEL, 2 * D_FF), D_MODEL),
        "ffn_w_down": nrm((DEPTH, 2, D_FF, D_MODEL), D_FF),
        "xa_w_q": nrm((DEPTH, D_MODEL, D_MODEL), D_MODEL),
        "xa_w_kv": nrm((DEPTH, D_MODEL, 2 * D_MODEL), D_MODEL),
        "xa_w_o": nrm((DEPTH, D_MODEL, D_MODEL), D_MODEL),
        "ev_w_in": nrm((N_EVEN, D_MODEL, EVEN_IN), D_MODEL),
        "ev_kv_norm": gain((N_EVEN, KV_RANK)),
        "ev_w_uk": nrm((N_EVEN, KV_RANK, A_WIDTH), KV_RANK),
        "ev_w_uv": nrm((N_EVEN, KV_RANK, A_WIDTH), KV_RANK),
        "ev_conv_w": nrm((N_EVEN, CONV_W, B_WIDTH), CONV_W),
        "ev_conv_b": small((N_EVEN, B_WIDTH)),
        "ev_w_ra": nrm((N_EVEN, B_BLOCKS, B_BLOCK_DIM, B_BLOCK_DIM), B_BLOCK_DIM),
        "ev_b_ra": small((N_EVEN, B_BLOCKS, B_BLOCK_DIM)),
        "ev_w_ri": nrm((N_EVEN, B_BLOCKS, B_BLOCK_DIM, B_BLOCK_DIM), B_BLOCK_DIM),
        "ev_b_ri": small((N_EVEN, B_BLOCKS, B_BLOCK_DIM)),
        "ev_lam": lam,
        "ev_w_out": nrm((N_EVEN, D_MODEL, D_MODEL), D_MODEL),
        "od_w_in": nrm((N_ODD, D_MODEL, ODD_IN), D_MODEL),
        "od_w_g2": nrm((N_ODD, GLA_GATE_RANK, GLA_DK), GLA_GATE_RANK),
        "od_b_g": small((N_ODD, GLA_DK), 0.1),
        "od_head_norm": gain((N_ODD, GLA_DVH)),
        "od_w_out": nrm((N_ODD, GLA_DV, D_MODEL), GLA_DV),
    }

def reference(x, mem, norms, ffn_w_gu, ffn_w_down, xa_w_q, xa_w_kv, xa_w_o,
              ev_w_in, ev_kv_norm, ev_w_uk, ev_w_uv, ev_conv_w, ev_conv_b, ev_w_ra, ev_b_ra,
              ev_w_ri, ev_b_ri, ev_lam, ev_w_out,
              od_w_in, od_w_g2, od_b_g, od_head_norm, od_w_out):
    h = x
    for layer in range(DEPTH):
        g = norms[layer]
        f = swiglu(rmsnorm(h, g[N_FFN1_PRE]), ffn_w_gu[layer, 0], ffn_w_down[layer, 0])
        h = h + 0.5 * rmsnorm(f, g[N_FFN1_POST])
        hn = rmsnorm(h, g[N_MIX_PRE])
        if layer % 2 == 0:
            e = layer // 2
            m = even_mixer(hn, ev_w_in[e], ev_kv_norm[e], ev_w_uk[e], ev_w_uv[e], ev_conv_w[e], ev_conv_b[e],
                           ev_w_ra[e], ev_b_ra[e], ev_w_ri[e], ev_b_ri[e], ev_lam[e], ev_w_out[e])
        else:
            o = layer // 2
            m = gla_mixer(hn, od_w_in[o], od_w_g2[o], od_b_g[o], od_head_norm[o], od_w_out[o])
        h = h + rmsnorm(m, g[N_MIX_POST])
        mem_n = rmsnorm(mem, g[N_MEM_NORM])
        c = mem_cross_attention(rmsnorm(h, g[N_XA_PRE]), mem_n, xa_w_q[layer], xa_w_kv[layer], xa_w_o[layer])
        h = h + rmsnorm(c, g[N_XA_POST])
        f = swiglu(rmsnorm(h, g[N_FFN2_PRE]), ffn_w_gu[layer, 1], ffn_w_down[layer, 1])
        h = h + 0.5 * rmsnorm(f, g[N_FFN2_POST])
    return h


_drawn_inputs = setup_inputs


def setup_inputs(seed=0):
    import zlib

    import numpy as np

    out = dict(_drawn_inputs(seed))
    spreads = {}
    factors = {'ev_kv_norm': 4.755,
     'ev_b_ra': 193.943,
     'ev_b_ri': 64.0,
     'od_head_norm': 200.0,
     'ev_conv_b': 6.86}
    for name, (base, spread) in spreads.items():
        noise = np.random.default_rng([zlib.crc32(name.encode()), seed]).standard_normal(out[name].shape)
        drawn = base * np.exp(spread * noise) if base else spread * noise
        out[name] = __import__('jax').numpy.asarray(drawn.astype(out[name].dtype))
    for name, factor in factors.items():
        out[name] = (out[name] * factor).astype(out[name].dtype)
    return out
```

```python
import numpy as np
import concourse.bass as bass
from concourse import mybir
from contextlib import ExitStack

DM, SEQ, NMEM = 1024, 512, 256
DFF = 2816
P = 128
KT = DM // P
TT = SEQ // P
FT = DFF // P
MT = NMEM // P
EPS = 1e-6
UB = 8
UW = UB * P
DU = -(-FT // UB)
XH, XD = 4, 256
AH, AD = 8, 64
IH, ID = 8, 64
TOPK = min(256, SEQ // 4)
RANK = 256
LRUT = 512 // P
CONV = 4
GH, GDK, GDV = 4, 128, 256
CH = 64
GR = 16

PARTS = [("ffn", 0, 0), ("even", 0, 0), ("cross", 0, 0), ("ffn", 0, 1),
         ("ffn", 1, 0), ("gla", 1, 0), ("cross", 1, 0), ("ffn", 1, 1)]
UNITS = {
    "ffn": [("gate_up", 2 * FT), ("down", DU * KT)],
    "even": [("q_idx", 4), ("c_kv", 2), ("kw_idx", 1), ("x_b", 4), ("uk", 1), ("uv", 1), ("gate", 4), ("q", 4),
             ("out", KT)],
    "cross": [("k", KT), ("v", KT), ("q", KT), ("out", KT)],
    "gla": [("g_lr", 1), ("q", 4), ("k", 4), ("v", KT), ("r", KT), ("out", KT)],
}
COLS = {}
_n = 0
for _name, _w in [("kv_norm", RANK // P), ("conv_w", LRUT * CONV), ("conv_b", LRUT),
                  ("b_ra", LRUT), ("b_ri", LRUT), ("lam", LRUT), ("b_g", GH), ("post", len(PARTS) * KT)]:
    COLS[_name] = _n
    _n += _w


def unit_starts(parts):
    at, n = {}, 0
    for i, (kind, _, _) in enumerate(parts):
        for seg, k in UNITS[kind]:
            at[i, seg] = n
            n += k
    return at, n


def trunk(nc, parts, x, mem, wstream, cols, gains, mem_gains, head_gain, w_ra, w_ri, w_g2, out):
    f32, f32r = mybir.dt.float32, mybir.dt.float32r
    ALU, ACT, AX = mybir.AluOpType, mybir.ActivationFunctionType, mybir.AxisListType
    U, _ = unit_starts(parts)
    NU = wstream.shape[0]
    NP = len(parts)

    ctx = ExitStack()
    with ctx:
        def sb(name, shape, dt=f32):
            return ctx.enter_context(nc.sbuf_tensor(name, shape, dt))

        def sem(name):
            return ctx.enter_context(nc.semaphore(name))

        h = sb("h", [P, TT, DM])
        f = sb("f", [P, TT, DM])
        x_hi = sb("x_hi", [P, KT, SEQ], f32r)
        x_lo = sb("x_lo", [P, KT, SEQ], f32r)
        w_raw = sb("w_raw", [P, 2, UW])
        w_hi = sb("w_hi", [P, 2, UW], f32r)
        w_lo = sb("w_lo", [P, 2, UW], f32r)
        tmp = sb("tmp", [P, 4, SEQ])
        gain_bc = sb("gain_bc", [P, DM])
        col = sb("col", [P, cols.shape[1]])
        ident = sb("ident", [P, P])
        ones = sb("ones", [P, P])
        eps = sb("eps", [P, 2])
        stat = sb("stat", [P, NP + 1, 32])
        with ExitStack() as own:
            def part_sb(name, shape, dt=f32):
                return own.enter_context(nc.sbuf_tensor(name, shape, dt))
            act_hi = part_sb("act_hi", [P, FT, SEQ], f32r)
            act_lo = part_sb("act_lo", [P, FT, SEQ], f32r)
        with ExitStack() as own:
            def part_sb(name, shape, dt=f32):
                return own.enter_context(nc.sbuf_tensor(name, shape, dt))
            c_mem = part_sb("c_mem", [P, MT, DM])
            c_gain = part_sb("c_gain", [P, DM])
            c_mem_hi = part_sb("c_mem_hi", [P, KT, NMEM], f32r)
            c_mem_lo = part_sb("c_mem_lo", [P, KT, NMEM], f32r)
            c_kT = part_sb("c_kT", [P, KT, NMEM])
            c_v = part_sb("c_v", [P, MT, DM])
            c_qT = part_sb("c_qT", [P, KT, SEQ])
            c_p = part_sb("c_p", [P, 3, NMEM])
            c_pT = part_sb("c_pT", [P, 2, MT, SEQ])
            c_stat = part_sb("c_stat", [P, 80])
        with ExitStack() as own:
            def part_sb(name, shape, dt=f32):
                return own.enter_context(nc.sbuf_tensor(name, shape, dt))
            e_k2 = part_sb("e_k2", [P, SEQ])
            e_wi = part_sb("e_wi", [IH, SEQ])
            e_w = part_sb("e_w", [P, TT, IH])
            e_kT = part_sb("e_kT", [P, 4, SEQ])
            e_v = part_sb("e_v", [P, TT, AH * AD])
            e_xc = part_sb("e_xc", [P, LRUT, SEQ])
            e_gate = part_sb("e_gate", [P, LRUT, SEQ])
            e_qT = part_sb("e_qT", [P, 4, SEQ])
            e_sc = part_sb("e_sc", [P, TT - 1, SEQ])
            e_tri = part_sb("e_tri", [P, P])
            e_bd = part_sb("e_bd", [P, 2, LRUT, P])
            e_max8 = part_sb("e_max8", [P, 8])
            e_lam = part_sb("e_lam", [P, 8, LRUT])
            e_st = part_sb("e_st", [P, 16])
            with ExitStack() as early:
                e_qi = early.enter_context(nc.sbuf_tensor("e_qi", [P, 4, SEQ], f32))
                e_ck = early.enter_context(nc.sbuf_tensor("e_ck", [P, 2, SEQ], f32))
                e_ck_hi = early.enter_context(nc.sbuf_tensor("e_ck_hi", [P, 2, SEQ], f32r))
                e_ck_lo = early.enter_context(nc.sbuf_tensor("e_ck_lo", [P, 2, SEQ], f32r))
                e_xb = early.enter_context(nc.sbuf_tensor("e_xb", [P, LRUT, SEQ + 4], f32))
            e_p = part_sb("e_p", [P, 3, SEQ])
            e_pT = part_sb("e_pT", [P, 2, TT, SEQ])
        with ExitStack() as own:
            def part_sb(name, shape, dt=f32):
                return own.enter_context(nc.sbuf_tensor(name, shape, dt))
            g_q = part_sb("g_q", [P, GH, SEQ])
            g_k = part_sb("g_k", [P, GH, SEQ])
            g_kr = part_sb("g_kr", [P, GH, SEQ])
            g_krt = part_sb("g_krt", [P, TT, GH, P])
            g_v = part_sb("g_v", [P, TT, DM])
            g_r = part_sb("g_r", [P, KT, SEQ])
            g_lr = part_sb("g_lr", [GR, SEQ])
            g_w2 = part_sb("g_w2", [GR, GH * GDK])
            g_t = part_sb("g_t", [P, 2, SEQ])
            g_S = part_sb("g_S", [P, GH, 3, GDV])
            g_dec = part_sb("g_dec", [P, GH, SEQ // CH])
            g_att = part_sb("g_att", [P, 2, P])
            g_mask = part_sb("g_mask", [P, P])
            g_gain = part_sb("g_gain", [P, GDV])
            g_st = part_sb("g_st", [P, 4, TT * GH])
            g_keep = part_sb("g_keep", [P, SEQ])
        ps = ctx.enter_context(nc.psum_tensor("ps", [P, 8, SEQ], f32))

        def bank(b):
            return ps[:, b, :]

        w_in = [sem("w_in0"), sem("w_in1")]
        w_hi_ready = sem("w_hi_ready")
        w_ready = sem("w_ready")
        w_free = sem("w_free")
        cols_in = sem("cols_in")
        x_in = [sem(f"x_in{t}") for t in range(TT)]
        gain_in = sem("gain_in")
        consts = sem("consts")
        ssq_ready = sem("ssq_ready")
        root_ready = sem("root_ready")
        h_ready = sem("h_ready")
        h_sq = sem("h_sq")
        xs_ready = sem("xs_ready")
        xT_ready = sem("xT_ready")
        x_hi_ready = sem("x_hi_ready")
        x_ready = sem("x_ready")
        stat_link = sem("stat_link")
        gu_free = sem("gu_free")
        silu_ready = sem("silu_ready")
        act_hi_ready = sem("act_hi_ready")
        act_ready = sem("act_ready")
        o_free = sem("o_free")
        oT_full = sem("oT_full")
        f_ready = sem("f_ready")
        p_free = sem("p_free")
        v_ready = sem("v_ready")
        mem_in = sem("mem_in")
        mem_sq = sem("mem_sq")
        mem_root = sem("mem_root")
        mem_n = sem("mem_n")
        memT_ready = sem("memT_ready")
        memT_hi = sem("memT_hi")
        memT_used = sem("memT_used")
        at_s = sem("at_s")
        at_sm = sem("at_sm")
        at_e = sem("at_e")
        at_p = sem("at_p")
        at_t = sem("at_t")
        at_pT = sem("at_pT")
        at_o = sem("at_o")
        at_ohi = sem("at_ohi")
        at_olo = sem("at_olo")
        out_done = sem("out_done")
        e_names = ["sq", "ssq", "ms", "rs", "ckn", "ck_hi", "ck_ready", "wT", "w", "s", "relu", "acc", "filled",
                   "uk_full", "tri", "bd0", "bd", "pad", "conv", "gates", "sig", "bv", "tanh", "exp", "sqrt",
                   "gelu", "t2", "y", "y_hi", "y_ready", "lam", "lam_abs", "lam_exp", "pool_link"]
        e = {n: sem("e_" + n) for n in e_names}
        g_names = ["lr", "z_full", "z", "abs", "exp", "ln", "G", "e", "qk", "krT", "krt", "att_full", "att", "u_full",
                   "S", "o_full", "o", "osq", "root", "on", "oT", "y", "y_hi", "y_ready", "w2_in", "gain_in",
                   "mask", "keep", "zero", "r"]
        gs = {n: sem("g_" + n) for n in g_names}

        block = ctx.enter_context(nc.Block())

        nffn = [sum(k == "ffn" for k, _, _ in parts[:i]) for i in range(NP)]
        ncross = [sum(k == "cross" for k, _, _ in parts[:i]) for i in range(NP)]
        PROJ = {"ffn": {}, "cross": {"k": KT, "q": KT},
                "even": {"q_idx": 4, "c_kv": 2, "kw_idx": 1, "x_b": 4, "uk": 4, "gate": 4, "q": 4},
                "gla": {"g_lr": 1, "q": 4, "k": 4, "r": KT}}
        PT0, n = {}, 0
        for i, (kind, _, _) in enumerate(parts):
            for seg, k in PROJ[kind].items():
                PT0[i, seg] = n
                n += k
        VG = {"ffn": 0, "cross": 2, "even": 1, "gla": 2}
        V0 = [sum(VG[k] for k, _, _ in parts[:i]) for i in range(NP)]
        ATI = {"ffn": 0, "cross": XH * TT, "even": AH * TT, "gla": 0}
        ATO = {"ffn": 0, "cross": XH * 2, "even": AH // 2, "gla": 0}
        A0 = [sum(ATI[k] for k, _, _ in parts[:i]) for i in range(NP)]
        O0 = [sum(ATO[k] for k, _, _ in parts[:i]) for i in range(NP)]

        def split_hi(act, v, s):
            act.wait_ge(w_in[s], (v // 2 + 1) * 16 if isinstance(v, int) else v * 8 + (16 if s == 0 else 8))
            act.wait_ge(w_free, v + 1)
            nc.scalar.activation(w_hi[:, s, :], w_raw[:, s, :], ACT.Copy).then_inc(w_hi_ready, 1)

        def split_lo(dve, v, s):
            dve.wait_ge(w_hi_ready, v + 1)
            nc.vector.tensor_tensor(w_lo[:, s, :], w_raw[:, s, :], w_hi[:, s, :].bitcast(f32), ALU.subtract)\
                .then_inc(w_ready, 1)

        def three(dst, wh, wl, xh, xl, start, stop):
            nc.tensor.matmul(dst, wh, xh, start=start, stop=False)
            nc.tensor.matmul(dst, wh, xl, start=False, stop=False)
            return nc.tensor.matmul(dst, wl, xh, start=False, stop=stop)

        def unit_tile(pe, v, s, dst, xh, xl, k0=0, nk=UB, start=True, stop=True, between=None):
            pe.wait_ge(w_ready, v + 1)
            for b in range(nk):
                if between is not None and b == UB // 2:
                    between()
                last = three(dst, w_hi[:, s, b * P:(b + 1) * P], w_lo[:, s, b * P:(b + 1) * P],
                             xh[:, k0 + b, :], xl[:, k0 + b, :], start and b == 0, stop and b == nk - 1)
            last.then_inc(w_free, 1)
            return last

        f_r = f[:, 0:2, :].rearrange("p a (b c) -> p (a b) c", c=SEQ)
        f_i = f[:, 2:4, :].rearrange("p a (b c) -> p (a b) c", c=SEQ)
        e_a = e_pT[:, 0, :, :]
        NEG, NOT_CAUSAL, TAKEN = -3.0e38, -3.4e38, -3.2e38

        def even_slots(g, o):
            return (g // 2, 4 + g // 2 % 2, g // 2) if g % 2 else None

        def cross_slots(g, o):
            return 2 * g + o, 4 + o, 2 * g + o

        @block.sync
        def _(sp):
            sp.dma_start(h[:, 1, :], x[P:2 * P, :]).then_inc(x_in[1], 16)
            sp.dma_start(h[:, 3, :], x[3 * P:4 * P, :]).then_inc(x_in[3], 16)
            sp.dma_start(w_raw[:, 0, :], wstream[0]).then_inc(w_in[0], 16)
            sp.dma_start(w_raw[:, 1, :], wstream[1]).then_inc(w_in[1], 16)
            with sp.Fori(1, NU // 2) as i:
                for s in range(2):
                    sp.wait_ge(w_ready, 2 * i + (s - 1))
                    sp.dma_start(w_raw[:, s:s + 1, :], wstream[bass.ds(2 * i + s, 1)].rearrange("o p c -> p o c"))\
                        .then_inc(w_in[s], 16)
            if NU % 2:
                sp.wait_ge(w_ready, NU - 2)
                sp.dma_start(w_raw[:, (NU - 1) % 2, :], wstream[NU - 1]).then_inc(w_in[(NU - 1) % 2], 16)
            for t in range(TT):
                sp.wait_ge(h_ready, TT * (NP - 1) + t + 1)
                sp.dma_start(out[t * P:(t + 1) * P, :], h[:, t, :]).then_inc(out_done, 16)
            sp.wait_ge(out_done, 16 * TT)

        @block.gpsimd
        def _(pool):
            nc.gpsimd.memset(ident[:, :], 0.0).then_inc(consts, 1)
            nc.gpsimd.memset(ones[:, :], 1.0).then_inc(consts, 1)
            nc.gpsimd.memset(eps[:, 0:1], EPS).then_inc(consts, 1)
            nc.gpsimd.memset(eps[:, 1:2], 4 * EPS).then_inc(consts, 1)
            pool.wait_ge(consts, 4)
            nc.gpsimd.affine_select(out=ident[:, :], in_=ident[:, :], compare_op=ALU.not_equal, fill=1.0,
                                    base=0, pattern=[[-1, P]], channel_multiplier=1).then_inc(consts, 1)

            def even(i):
                count = [0]

                def link(ins):
                    count[0] += 1
                    ins.then_inc(e["pool_link"], 1)
                    pool.wait_ge(e["pool_link"], count[0])

                nc.gpsimd.memset(e_bd[:, :, :, :], 0.0).then_inc(e["bd0"], 1)
                nc.gpsimd.memset(e_xb[:, :, 0:CONV - 1], 0.0).then_inc(e["pad"], 1)
                link(nc.gpsimd.memset(e_tri[:, :], 0.0))
                nc.gpsimd.affine_select(out=e_tri[:, :], in_=e_tri[:, :], compare_op=ALU.is_ge, fill=NEG, base=0,
                                        pattern=[[-1, P]], channel_multiplier=1).then_inc(e["tri"], 1)
                for b in range(1, TT):
                    pool.wait_ge(e["acc"], IH * b)
                    diag = e_sc[:, b - 1, b * P:(b + 1) * P]
                    nc.gpsimd.affine_select(out=diag, in_=diag, compare_op=ALU.is_ge, fill=NOT_CAUSAL, base=0,
                                            pattern=[[-1, P]], channel_multiplier=1).then_inc(e["filled"], 1)
                for c in range(LRUT):
                    pool.wait_ge(p_free, PT0[i, "x_b"] + c + 3)
                    w0 = COLS["conv_w"] + c * CONV
                    b0 = COLS["conv_b"] + c
                    for k in range(CONV):
                        if k == 0:
                            link(nc.gpsimd.tensor_scalar(e_xc[:, c, :], e_xb[:, c, 0:SEQ], col[:, w0:w0 + 1],
                                                         col[:, b0:b0 + 1], ALU.mult, ALU.add))
                        else:
                            link(nc.gpsimd.tensor_scalar(tmp[:, 3, :], e_xb[:, c, k:k + SEQ],
                                                         col[:, w0 + k:w0 + k + 1], None, ALU.mult))
                            ins = nc.gpsimd.tensor_tensor(e_xc[:, c, :], e_xc[:, c, :], tmp[:, 3, :], ALU.add)
                            if k < CONV - 1:
                                link(ins)
                            else:
                                ins.then_inc(e["conv"], 1)
                for c in range(LRUT):
                    pool.wait_ge(e["sig"], 2 * LRUT)
                    nc.gpsimd.tensor_tensor(e_xc[:, c, :], e_xc[:, c, :], f_i[:, c, :], ALU.mult)\
                        .then_inc(e["t2"], 1)

            def gla(i):
                nc.gpsimd.memset(g_keep[:, :], 1.0).then_inc(gs["keep"], 1)
                pool.wait_ge(gs["keep"], 1)
                nc.gpsimd.memset(g_keep[:, :].rearrange("p (c t) -> p c t", t=CH)[:, :, 0:1], 0.0)\
                    .then_inc(gs["keep"], 1)
                nc.gpsimd.memset(g_mask[:, :], 1.0).then_inc(gs["mask"], 1)
                pool.wait_ge(gs["mask"], 1)
                nc.gpsimd.affine_select(out=g_mask[:, :], in_=g_mask[:, :], compare_op=ALU.is_ge, fill=0.0, base=0,
                                        pattern=[[1, P]], channel_multiplier=-1).then_inc(gs["mask"], 1)
                pool.wait_ge(gs["mask"], 2)
                nc.gpsimd.memset(g_mask[0:CH, CH:P], 0.0).then_inc(gs["mask"], 1)
                nc.gpsimd.memset(g_att[:, :, :], 0.0).then_inc(gs["zero"], 1)

            for i in range(NP):
                if i > 0 and parts[i][0] in ("even", "gla"):
                    pool.wait_ge(h_ready, TT * i)
                if parts[i][0] == "even":
                    even(i)
                elif parts[i][0] == "gla":
                    gla(i)

        @block.scalar
        def _(act):
            nc.scalar.dma_start(h[:, 0, :], x[0:P, :]).then_inc(x_in[0], 16)
            nc.scalar.dma_start(gain_bc[:, :], gains[0:1, :].to_broadcast([P, DM])).then_inc(gain_in, 16)
            nc.scalar.dma_start(h[:, 2, :], x[2 * P:3 * P, :]).then_inc(x_in[2], 16)
            nc.scalar.dma_start(col[:, :], cols).then_inc(cols_in, 16)
            act.sem_inc(o_free, 2)
            act.sem_inc(p_free, 2)

            def post_root(i):
                half = parts[i - 1][0] == "ffn"
                act.wait_ge(ssq_ready, i)
                nc.scalar.activation(stat[:, i, 4:8], stat[:, i, 0:4], ACT.Sqrt, scale=(4.0 if half else 1.0) / DM,
                                     bias=eps[:, 1:2] if half else eps[:, 0:1]).then_inc(root_ready, 1)

            def norm(i):
                if i == 0:
                    act.wait_ge(consts, 5)
                else:
                    post_root(i)

                def root(t):
                    act.wait_ge(h_sq, TT * i + t + 1)
                    nc.scalar.activation(stat[:, i, 16 + t:17 + t], stat[:, i, 12 + t:13 + t], ACT.Sqrt,
                                         scale=1.0 / DM, bias=eps[:, 0:1]).then_inc(root_ready, 1)

                def square(t):
                    if i > 0:
                        act.wait_ge(h_ready, TT * (i - 1) + t + 1)
                    else:
                        act.wait_ge(x_in[t], 16)
                    if i + t > 0:
                        act.wait_ge(h_sq, TT * i + t)
                    nc.scalar.activation(tmp[:, 0:2, :].rearrange("p a b -> p (a b)"), h[:, t, :], ACT.Square,
                                         accum_out=stat[:, i, 12 + t:13 + t]).then_inc(h_sq, 1)

                def upper(t):
                    for b in range(2):
                        act.wait_ge(xT_ready, 2 * TT * i + 2 * t + b + 1)
                        nc.scalar.activation(x_hi[:, 4 * b:4 * b + 4, t * P:(t + 1) * P],
                                             bank(4 + 2 * (t % 2) + b).rearrange("p (k c) -> p k c", k=4),
                                             ACT.Copy).then_inc(x_hi_ready, 1)
                def key(k):
                    u = U[i, "k"] + k
                    act.wait_ge(w_free, u + 3)
                    nc.scalar.activation(c_kT[:, k, :], bank((PT0[i, "k"] + k) % 2)[:, 0:NMEM], ACT.Copy)\
                        .then_inc(p_free, 1)
                    split_hi(act, u + 2, u % 2)

                if parts[i][0] == "cross":
                    square(0)
                    key(0)
                    square(1)
                    root(0)
                    key(1)
                    square(2)
                    root(1)
                    key(2)
                    upper(0)
                    key(3)
                    square(3)
                    root(2)
                    key(4)
                    upper(1)
                    root(3)
                    key(5)
                    key(6)
                    upper(2)
                    key(7)
                    split_units(i, "v", 2)
                    upper(3)
                else:
                    square(0)
                    square(1)
                    root(0)
                    square(2)
                    root(1)
                    upper(0)
                    square(3)
                    root(2)
                    upper(1)
                    root(3)
                    if i == 0:
                        split_hi(act, 0, 0)
                    upper(2)
                    if i == 0:
                        split_hi(act, 1, 1)
                    upper(3)
                if i == 0:
                    act.wait_ge(cols_in, 16)
                if i + 1 < NP:
                    act.wait_ge(xs_ready, TT * (i + 1))
                    nc.scalar.dma_start(gain_bc[:, :], gains[i + 1:i + 2, :].to_broadcast([P, DM]))\
                        .then_inc(gain_in, 16)

            def ffn(i):
                n0, u0 = nffn[i] * FT, U[i, "gate_up"]
                act.preload_act_table(ACT.Silu)
                with act.Fori(0, FT // 2) as it:
                    for jj in range(2):
                        j = 2 * it + jj
                        split_hi(act, 2 * j + (u0 + 2), u0 % 2)
                        act.wait_ge(w_free, 2 * j + (u0 + 4))
                        act.wait_ge(act_ready, j + (n0 + 1))
                        nc.scalar.activation(tmp[:, jj, :], bank(2 * jj), ACT.Silu).then_inc(silu_ready, 1)
                        split_hi(act, 2 * j + (u0 + 3), (u0 + 1) % 2)
                        act.wait_ge(gu_free, j + (n0 + 3))
                        nc.scalar.activation(act_hi[:, bass.ds(j, 1), :], tmp[:, jj:jj + 1, :], ACT.Copy)\
                            .then_inc(act_hi_ready, 1)
                output(i, "down", DU)

            def mem_load(i):
                layer = parts[i + 1][1]
                if parts[i][0] == "even":
                    act.wait_ge(at_olo, O0[i] + AH // 2)
                else:
                    act.wait_ge(gs["y_ready"], 2 * TT)
                nc.scalar.dma_start(c_mem[:, :, :], mem.rearrange("(m p) d -> p m d", p=P)).then_inc(mem_in, 16)
                nc.scalar.dma_start(c_gain[:, :], mem_gains[layer:layer + 1, :].to_broadcast([P, DM]))\
                    .then_inc(mem_in, 16)

            def mem_norm(i):
                c = ncross[i + 1]
                act.wait_ge(mem_in, 32 * (c + 1))
                for m in range(MT):
                    nc.scalar.activation(c_v[:, m, :], c_mem[:, m, :], ACT.Square, accum_out=c_stat[:, m:m + 1])\
                        .then_inc(mem_sq, 1)
                act.wait_ge(mem_sq, MT * (c + 1))
                nc.scalar.activation(c_stat[:, 4:4 + MT], c_stat[:, 0:MT], ACT.Sqrt, scale=1.0 / DM,
                                     bias=eps[:, 0:1]).then_inc(mem_root, 1)

            def mem_upper(i):
                c = ncross[i + 1]
                for m in range(MT):
                    for b in range(2):
                        act.wait_ge(memT_ready, 4 * c + 2 * m + b + 1)
                        nc.scalar.activation(c_mem_hi[:, 4 * b:4 * b + 4, m * P:(m + 1) * P],
                                             bank(2 * m + b).rearrange("p (k c) -> p k c", k=4), ACT.Copy)\
                            .then_inc(memT_hi, 1)

            def output(i, seg, per):
                u0 = U[i, seg]
                mem_next = i + 1 < NP and parts[i + 1][0] == "cross"
                if mem_next:
                    mem_load(i)

                def tile(n, s0, nn, kk):
                    v = n * per + u0
                    for q in range(per - 1):
                        if nn is None or v + q + 2 < NU:
                            split_hi(act, v + (q + 2), (s0 + q) % 2)
                    act.wait_ge(w_free, v + (per + 2))
                    act.wait_ge(oT_full, n + (KT * i + 1))
                    c0 = COLS["post"] + i * KT
                    nc.scalar.activation(tmp[:, kk, :], bank(4 + kk), ACT.Copy, scale=col[:, bass.ds(n + c0, 1)])
                    nc.scalar.activation(tmp[:, 2 + kk, :], bank(4 + kk), ACT.Square).then_inc(o_free, 1)
                    if nn is None or v + per + 1 < NU:
                        split_hi(act, v + (per + 1), (s0 + per - 1) % 2)

                tile(0, u0 % 2, 0, 0)
                for first, end in ((0, 1), (1, KT // 2 - 1)) if mem_next else ((0, KT // 2 - 1),):
                    with act.Fori(first, end) as it:
                        tile(2 * it + 1, (u0 + per) % 2, None, 1)
                        tile(2 * it + 2, u0 % 2, None, 0)
                    if mem_next:
                        mem_norm(i) if first == 0 else mem_upper(i)
                tile(KT - 1, (u0 + per * (KT - 1)) % 2, KT - 1, 1)

            def project(i, seg, n, dst, w=SEQ, func=ACT.Copy, at=0):
                u0, t0 = U[i, seg], PT0[i, seg]
                with act.Fori(0, n // 2) as it:
                    for jj in range(2):
                        j = 2 * it + jj
                        act.wait_ge(w_free, j + (u0 + 3))
                        nc.scalar.activation(dst[:, bass.ds(j, 1), at:at + w],
                                             ps[:, (t0 + jj) % 2:(t0 + jj) % 2 + 1, 0:w], func).then_inc(p_free, 1)
                        split_hi(act, j + (u0 + 2), (u0 + jj) % 2)

            def split_units(i, seg, n, off=0):
                for q in range(n):
                    v = U[i, seg] + off + q + 2
                    split_hi(act, v, v % 2)

            def attend(i, heads, p, st, scale, slots, out_banks, nk, direct):
                a0, o0 = A0[i], O0[i]
                N = heads * TT
                for step in range(N + 1):
                    if step < N:
                        act.wait_ge(at_sm, a0 + step + 1)
                        c = (step % 4) * 4
                        w = nk(step % TT) * P
                        dst = p[:, step % 3, 0:w]
                        nc.scalar.activation(dst, bank(step % 2)[:, 0:w] if direct else dst,
                                             ACT.Exp, bias=st[:, c + 1:c + 2], scale=scale,
                                             accum_out=st[:, c + 2:c + 3]).then_inc(at_e, 1)
                    if step > 0 and (step - 1) % TT == 1 and (step - 1) // TT >= 1:
                        g = (step - 1) // TT - 1
                        for o in range(out_banks):
                            if slots(g, o) is not None:
                                upper_out(i, g, o, slots)
                g = heads - 1
                for o in range(out_banks):
                    if slots(g, o) is not None:
                        upper_out(i, g, o, slots)

            def upper_out(i, g, o, slots):
                k, b, idx = slots(g, o)
                act.wait_ge(at_o, O0[i] + idx + 1)
                nc.scalar.activation(x_hi[:, k, :], bank(b), ACT.Copy).then_inc(at_ohi, 1)

            def cross(i):
                for hf in range(2):
                    split_units(i, "v", 4 - 2 * (1 - hf), 4 * hf + 2 * (1 - hf))
                    act.wait_ge(w_free, U[i, "v"] + 4 * hf + 6)
                    nc.scalar.activation(c_v[:, :, hf * SEQ:(hf + 1) * SEQ], ps[:, 2 - 2 * hf:4 - 2 * hf, :], ACT.Copy)\
                        .then_inc(v_ready, 1)
                act.preload_act_table(ACT.Exp)
                project(i, "q", KT, c_qT)
                attend(i, XH, c_p, c_stat[:, 8:32], XD ** -0.5, cross_slots, 2, lambda t: MT, True)
                output(i, "out", 1)

            def even(i):
                u0 = U[i, "q_idx"]
                act.wait_ge(e["bd0"], 1)
                for n, w in enumerate((w_ra, w_ri)):
                    for q in range(2):
                        nc.scalar.dma_start(e_bd[q * CH:(q + 1) * CH, n, :, q * CH:(q + 1) * CH],
                                            w.rearrange("(c q) i j -> q i c j", q=2)[q]).then_inc(e["bd"], 16)
                act.preload_act_table(ACT.Exp)
                lam = col[:, COLS["lam"]:COLS["lam"] + LRUT]
                nc.scalar.activation(e_lam[:, 0, :], lam, ACT.Abs).then_inc(e["lam_abs"], 1)
                act.wait_ge(e["lam_abs"], 1)
                nc.scalar.activation(e_lam[:, 1, :], e_lam[:, 0, :], ACT.Exp, scale=-1.0).then_inc(e["lam_exp"], 1)
                project(i, "q_idx", 4, e_qi)
                project(i, "c_kv", 2, e_ck)
                act.wait_ge(p_free, PT0[i, "c_kv"] + 4)
                for k in range(2):
                    nc.scalar.activation(tmp[:, k, :], e_ck[:, k, :], ACT.Square).then_inc(e["sq"], 1)
                act.wait_ge(w_free, U[i, "kw_idx"] + 3)
                b = PT0[i, "kw_idx"] % 2
                nc.scalar.activation(e_k2[0:ID, :], bank(b)[0:ID, :], ACT.Copy)
                nc.scalar.activation(e_k2[ID:2 * ID, :], bank(b)[0:ID, :], ACT.Copy)
                nc.scalar.activation(e_wi[:, :], bank(b)[ID:ID + IH, :], ACT.Copy).then_inc(p_free, 1)
                split_units(i, "kw_idx", 1)
                act.wait_ge(e["ms"], 1)
                nc.scalar.activation(tmp[:, 3, :], tmp[:, 2, :], ACT.Sqrt).then_inc(e["rs"], 1)
                for k in range(2):
                    act.wait_ge(e["ckn"], k + 1)
                    nc.scalar.activation(e_ck_hi[:, k, :], e_ck[:, k, :], ACT.Copy).then_inc(e["ck_hi"], 1)
                for n in range((TT - 1) * IH):
                    w = (n // IH + 2) * P
                    act.wait_ge(e["s"], n + 1)
                    if n >= 2:
                        act.wait_ge(e["acc"], n - 1)
                    nc.scalar.activation(tmp[:, n % 2, 0:w], bank(2 + n % 2)[:, 0:w], ACT.Relu).then_inc(e["relu"], 1)
                act.wait_ge(e["pad"], 1)
                project(i, "x_b", 4, e_xb, at=CONV - 1)
                for n in range(4):
                    if n < 3:
                        act.wait_ge(e["uk_full"], n + 1)
                    else:
                        act.wait_ge(w_free, U[i, "uk"] + 3)
                    nc.scalar.activation(e_kT[:, n, :], bank((PT0[i, "uk"] + n) % 2), ACT.Copy).then_inc(p_free, 1)
                split_units(i, "uk", 2)
                act.wait_ge(w_free, U[i, "uv"] + 3)
                nc.scalar.activation(e_v[:, :, :], ps[:, 4:8, :], ACT.Copy).then_inc(v_ready, 1)
                project(i, "gate", 4, e_gate)
                project(i, "q", 4, e_qT)
                act.preload_act_table(ACT.Sigmoid)
                for n, (dst, bias) in enumerate(((f_r, COLS["b_ra"]), (f_i, COLS["b_ri"]))):
                    for c in range(LRUT):
                        act.wait_ge(e["gates"], n * LRUT + c + 1)
                        nc.scalar.activation(dst[:, c, :], bank(4 * (1 - n) + c), ACT.Sigmoid,
                                             bias=col[:, bias + c:bias + c + 1]).then_inc(e["sig"], 1)
                act.preload_act_table(ACT.Exp)
                act.wait_ge(e["lam"], 1)
                act.wait_ge(e["conv"], LRUT)
                for c in range(LRUT):
                    act.wait_ge(e["sig"], c + 1)
                    nc.scalar.activation(tmp[:, c, :], f_r[:, c, :], ACT.Exp, scale=e_lam[:, 7, c:c + 1])\
                        .then_inc(e["exp"], 1)
                    act.wait_ge(e["exp"], c + 1)
                    nc.scalar.activation(f_r[:, c, :], f_r[:, c, :], ACT.Tanh, scale=e_lam[:, 6, c:c + 1])\
                        .then_inc(e["tanh"], 1)
                for c in range(LRUT):
                    act.wait_ge(e["bv"], c + 1)
                    act.wait_ge(e["tanh"], LRUT)
                    nc.scalar.activation(f_r[:, c, :], f_r[:, c, :], ACT.Sqrt, scale=4.0).then_inc(e["sqrt"], 1)
                for c in range(LRUT):
                    nc.scalar.activation(e_gate[:, c, :], e_gate[:, c, :], ACT.Gelu_apprx_tanh).then_inc(e["gelu"], 1)
                act.preload_act_table(ACT.Exp)
                for c in range(LRUT):
                    act.wait_ge(e["y"], c + 1)
                    nc.scalar.activation(x_hi[:, 4 + c, :], e_xc[:, c, :], ACT.Copy).then_inc(e["y_hi"], 1)
                attend(i, AH, e_p, e_st, AD ** -0.5, even_slots, 1, lambda t: t + 1, False)
                output(i, "out", 1)

            def gla(i):
                nc.scalar.dma_start(g_w2[:, :], w_g2).then_inc(gs["w2_in"], 16)
                nc.scalar.dma_start(g_gain[:, :], head_gain.to_broadcast([P, GDV])).then_inc(gs["gain_in"], 16)
                act.preload_act_table_set("natural_log_exp_and_others")
                act.wait_ge(w_free, U[i, "g_lr"] + 3)
                nc.scalar.activation(g_lr[:, :], bank(PT0[i, "g_lr"] % 2)[0:GR, :], ACT.Copy).then_inc(p_free, 1)
                split_units(i, "g_lr", 1)
                project(i, "q", GH, g_q)
                for n in range(GH):
                    c = COLS["b_g"] + n
                    act.wait_ge(gs["z_full"], n + 1)
                    nc.scalar.activation(g_kr[:, n, :], bank(4 + n), ACT.Identity, bias=col[:, c:c + 1])\
                        .then_inc(gs["z"], 1)
                project(i, "k", GH, g_k)
                act.wait_ge(p_free, PT0[i, "k"] + GH + 2)
                act.preload_act_table_set("natural_log_exp_and_others")
                for n in range(GH):
                    split_units(i, "v", 1, 2 * n)
                    act.wait_ge(gs["z"], n + 1)
                    if n > 0:
                        act.wait_ge(gs["G"], 2 * n)
                    nc.scalar.activation(tmp[:, 0, :], g_kr[:, n, :], ACT.Abs).then_inc(gs["abs"], 1)
                    act.wait_ge(gs["abs"], n + 1)
                    nc.scalar.activation(tmp[:, 0, :], tmp[:, 0, :], ACT.Exp, scale=-1.0).then_inc(gs["exp"], 1)
                    act.wait_ge(gs["exp"], n + 1)
                    nc.scalar.activation(tmp[:, 0, :], tmp[:, 0, :], ACT.Ln, bias=1.0).then_inc(gs["ln"], 1)
                    if n == 2:
                        act.wait_ge(w_free, U[i, "v"] + 6)
                        nc.scalar.activation(g_v[:, :, 0:SEQ], ps[:, 4:8, :], ACT.Copy).then_inc(v_ready, 1)
                    act.wait_ge(gs["G"], 2 * n + 2)
                    if n > 0:
                        act.wait_ge(gs["qk"], 3 * n)
                    nc.scalar.activation(g_t[:, 0, :], tmp[:, 2, :], ACT.Exp, scale=1.0 / 16)
                    nc.scalar.activation(g_t[:, 1, :], tmp[:, 2, :], ACT.Exp, scale=-1.0 / 16).then_inc(gs["e"], 1)
                    nc.scalar.activation(tmp[:, 3, :], tmp[:, 3, :], ACT.Exp, scale=1.0 / 16).then_inc(gs["e"], 1)
                    split_units(i, "v", 1, 2 * n + 1)
                act.wait_ge(w_free, U[i, "v"] + 10)
                nc.scalar.activation(g_v[:, :, SEQ:2 * SEQ], ps[:, 0:4, :], ACT.Copy).then_inc(v_ready, 1)
                for n in range(GH):
                    act.wait_ge(gs["krT"], n + 1)
                    nc.scalar.activation(g_krt[:, :, n, :], bank(4 + n).rearrange("p (t c) -> p t c", t=TT), ACT.Copy)\
                        .then_inc(gs["krt"], 1)
                act.preload_act_table(ACT.Silu)
                project(i, "r", KT, g_r, func=ACT.Silu)
                for w in range(TT * GH):
                    T, n = w // GH, w % GH
                    act.wait_ge(gs["o_full"], w + 1)
                    nc.scalar.activation(f[:, T, n * GDV:(n + 1) * GDV], bank(4 + w % 2)[:, 0:GDV], ACT.Copy)
                    if w > 0:
                        act.wait_ge(gs["osq"], w)
                    nc.scalar.activation(tmp[:, 2, 0:GDV], bank(4 + w % 2)[:, 0:GDV], ACT.Square,
                                         accum_out=g_st[:, 0, w:w + 1]).then_inc(gs["osq"], 1)
                    if n == GH - 1:
                        act.wait_ge(gs["osq"], w + 1)
                        nc.scalar.activation(g_st[:, 3, GH * T:GH * (T + 1)], g_st[:, 0, GH * T:GH * (T + 1)],
                                             ACT.Sqrt, scale=1.0 / GDV, bias=eps[:, 0:1]).then_inc(gs["root"], 1)
                for T in range(TT):
                    for b in range(2):
                        act.wait_ge(gs["y"], 2 * T + b + 1)
                        nc.scalar.activation(x_hi[:, 4 * b:4 * b + 4, T * P:(T + 1) * P],
                                             tmp[:, 2 * (T % 2) + b, :].rearrange("p (k c) -> p k c", k=4), ACT.Copy)\
                            .then_inc(gs["y_hi"], 1)
                output(i, "out", 1)

            for i in range(NP):
                norm(i)
                if parts[i][0] == "ffn":
                    ffn(i)
                elif parts[i][0] == "cross":
                    cross(i)
                elif parts[i][0] == "even":
                    even(i)
                else:
                    gla(i)
            post_root(NP)

        @block.vector
        def _(dve):
            dve.sem_inc(gu_free, 2)
            dve.sem_inc(act_ready, 2)
            dve.sem_inc(f_ready, 1)
            link_count = [0]

            def link(ins):
                link_count[0] += 1
                ins.then_inc(stat_link, 1)
                dve.wait_ge(stat_link, link_count[0])

            def norm(i):
                if i > 0:
                    nc.vector.tensor_reduce(stat[:, i, 0:TT], bank(7)[:, 0:KT * TT]
                                            .rearrange("p (n t) -> p t n", t=TT), AX.X, ALU.add)\
                        .then_inc(ssq_ready, 1)
                    dve.wait_ge(ssq_ready, i)
                    half = 4.0 if parts[i - 1][0] == "ffn" else 1.0
                    link(nc.vector.tensor_scalar(stat[:, i, 8:12], stat[:, i, 0:4], half / DM, half * EPS,
                                                 ALU.mult, ALU.add))
                    link(nc.vector.reciprocal(stat[:, i, 8:12], stat[:, i, 8:12]))
                    dve.wait_ge(root_ready, 5 * i)
                    link(nc.vector.tensor_tensor(stat[:, i, 8:12], stat[:, i, 8:12], stat[:, i, 4:8], ALU.mult))

                def update(t):
                    if i > 0:
                        nc.vector.scalar_tensor_tensor(h[:, t, :], f[:, t, :], stat[:, i, 8 + t:9 + t], h[:, t, :],
                                                       ALU.mult, ALU.add).then_inc(h_ready, 1)

                def mean(t):
                    dve.wait_ge(h_sq, TT * i + t + 1)
                    inv = stat[:, i, 20 + t:21 + t]
                    link(nc.vector.tensor_scalar(inv, stat[:, i, 12 + t:13 + t], 1.0 / DM, EPS, ALU.mult, ALU.add))
                    link(nc.vector.reciprocal(inv, inv))

                def scale(t):
                    dve.wait_ge(root_ready, 5 * i + t + 1)
                    inv = stat[:, i, 20 + t:21 + t]
                    link(nc.vector.tensor_tensor(inv, inv, stat[:, i, 16 + t:17 + t], ALU.mult))
                    if t == 0:
                        dve.wait_ge(gain_in, 16 * (i + 1))
                    if i == 0:
                        dve.wait_ge(x_in[t], 16)
                    nc.vector.scalar_tensor_tensor(f[:, t, :], h[:, t, :], stat[:, i, 20 + t:21 + t], gain_bc[:, :],
                                                   ALU.mult, ALU.mult).then_inc(xs_ready, 1)

                def lower(t):
                    for b in range(2):
                        dve.wait_ge(x_hi_ready, 2 * TT * i + 2 * t + b + 1)
                        xh = x_hi[:, 4 * b:4 * b + 4, t * P:(t + 1) * P]
                        nc.vector.tensor_tensor(x_lo[:, 4 * b:4 * b + 4, t * P:(t + 1) * P],
                                                bank(4 + 2 * (t % 2) + b).rearrange("p (k c) -> p k c", k=4),
                                                xh.bitcast(f32), ALU.subtract).then_inc(x_ready, 1)

                update(0)
                if i == NP:
                    for t in range(1, TT):
                        update(t)
                    return
                update(1)
                if i > 0:
                    v = U[i, UNITS[parts[i][0]][0][0]] + 1
                    split_lo(dve, v, v % 2)
                mean(0)
                scale(0)
                if parts[i][0] == "cross":
                    def keys(k, n):
                        for q in range(k, k + n):
                            split_lo(dve, U[i, "k"] + q + 2, (U[i, "k"] + q) % 2)

                    keys(0, 1)
                    update(2)
                    mean(1)
                    scale(1)
                    keys(1, 1)
                    lower(0)
                    keys(2, 1)
                    update(3)
                    mean(2)
                    keys(3, 1)
                    scale(2)
                    lower(1)
                    keys(4, 1)
                    mean(3)
                    scale(3)
                    keys(5, 2)
                    lower(2)
                    keys(7, 3)
                    lower(3)
                    return
                update(2)
                mean(1)
                scale(1)
                lower(0)
                update(3)
                mean(2)
                scale(2)
                lower(1)
                mean(3)
                scale(3)
                if i == 0:
                    split_lo(dve, 0, 0)
                lower(2)
                if i == 0:
                    split_lo(dve, 1, 1)
                lower(3)

            def ffn(i):
                n0, u0 = nffn[i] * FT, U[i, "gate_up"]
                with dve.Fori(0, FT // 2) as it:
                    for jj in range(2):
                        j = 2 * it + jj
                        split_lo(dve, 2 * j + (u0 + 2), u0 % 2)
                        dve.wait_ge(silu_ready, j + (n0 + 1))
                        nc.vector.tensor_tensor(tmp[:, jj, :], bank(2 * jj + 1), tmp[:, jj, :], ALU.mult)\
                            .then_inc(gu_free, 1)
                        split_lo(dve, 2 * j + (u0 + 3), (u0 + 1) % 2)
                        dve.wait_ge(act_hi_ready, j + (n0 + 1))
                        nc.vector.tensor_tensor(act_lo[:, bass.ds(j, 1), :], tmp[:, jj:jj + 1, :],
                                                act_hi[:, bass.ds(j, 1), :].bitcast(f32), ALU.subtract)\
                            .then_inc(act_ready, 1)
                output(i, "down", DU)

            def mem_norm(i):
                c = ncross[i + 1]
                dve.wait_ge(mem_sq, MT * (c + 1))
                inv = c_stat[:, 2:2 + MT]
                link(nc.vector.tensor_scalar(inv, c_stat[:, 0:MT], 1.0 / DM, EPS, ALU.mult, ALU.add))
                link(nc.vector.reciprocal(inv, inv))
                dve.wait_ge(mem_root, c + 1)
                link(nc.vector.tensor_tensor(inv, inv, c_stat[:, 4:4 + MT], ALU.mult))
                for m in range(MT):
                    nc.vector.scalar_tensor_tensor(c_mem[:, m, :], c_mem[:, m, :], c_stat[:, 2 + m:3 + m],
                                                   c_gain[:, :], ALU.mult, ALU.mult).then_inc(mem_n, 1)

            def mem_lower(i):
                c = ncross[i + 1]
                for m in range(MT):
                    for b in range(2):
                        dve.wait_ge(memT_hi, 4 * c + 2 * m + b + 1)
                        nc.vector.tensor_tensor(c_mem_lo[:, 4 * b:4 * b + 4, m * P:(m + 1) * P],
                                                bank(2 * m + b).rearrange("p (k c) -> p k c", k=4),
                                                c_mem_hi[:, 4 * b:4 * b + 4, m * P:(m + 1) * P].bitcast(f32),
                                                ALU.subtract).then_inc(memT_used, 1)

            def output(i, seg, per):
                u0 = U[i, seg]
                mem_next = i + 1 < NP and parts[i + 1][0] == "cross"

                def store(n):
                    dve.wait_ge(oT_full, n + (KT * i + 3))
                    dst = f[:, :, n * P:(n + 1) * P] if isinstance(n, int) else f[:, :, bass.ds(n * P, P)]
                    nc.vector.tensor_copy(dst, bank(6).rearrange("p (t c) -> p t c", t=TT)).then_inc(f_ready, 1)

                def tile(n, s0, stored, split_last=True):
                    v = n * per + u0
                    if stored is not None:
                        store(stored)
                    for q in range(per if split_last else per - 1):
                        if not isinstance(v, int) or v + q + 2 < NU:
                            split_lo(dve, v + (q + 2), (s0 + q) % 2)

                tile(0, u0 % 2, None)
                for first, end in ((0, 1), (1, KT // 2 - 1)) if mem_next else ((0, KT // 2 - 1),):
                    with dve.Fori(first, end) as it:
                        tile(2 * it + 1, (u0 + per) % 2, 2 * it)
                        tile(2 * it + 2, u0 % 2, 2 * it + 1)
                    if mem_next:
                        mem_norm(i) if first == 0 else mem_lower(i)
                tile(KT - 1, (u0 + per * (KT - 1)) % 2, KT - 2, False)
                store(KT - 1)

            def project(i, seg, n):
                u0 = U[i, seg]
                with dve.Fori(0, n // 2) as it:
                    for jj in range(2):
                        split_lo(dve, 2 * it + (u0 + 2 + jj), (u0 + jj) % 2)

            def split_units(i, seg, n, off=0):
                for q in range(n):
                    v = U[i, seg] + off + q + 2
                    split_lo(dve, v, v % 2)

            def attend(i, heads, p, pT, st, scale, slots, out_banks, nk, bias):
                a0 = A0[i]
                N = heads * TT

                def lower_out(g):
                    for o in range(out_banks):
                        if slots(g, o) is not None:
                            k, b, idx = slots(g, o)
                            dve.wait_ge(at_ohi, O0[i] + idx + 1)
                            nc.vector.tensor_tensor(x_lo[:, k, :], bank(b), x_hi[:, k, :].bitcast(f32), ALU.subtract)\
                                .then_inc(at_olo, 1)

                for step in range(N + 2):
                    if step < N:
                        w = nk(step % TT) * P
                        c = (step % 4) * 4
                        dve.wait_ge(at_s, a0 + step + 1)
                        if step >= 3:
                            dve.wait_ge(at_t, a0 + step - 2)
                        if bias is None:
                            link(nc.vector.tensor_reduce(st[:, c:c + 1], bank(step % 2)[:, 0:w], AX.X, ALU.max))
                        else:
                            link(nc.vector.tensor_tensor_reduce(
                                out=p[:, step % 3, 0:w], in0=bank(step % 2)[:, 0:w], in1=bias(step % TT),
                                scale=1.0, scalar=-3.0e38, op0=ALU.add, op1=ALU.max, accum_out=st[:, c:c + 1]))
                        nc.vector.tensor_scalar(st[:, c + 1:c + 2], st[:, c:c + 1], -scale, None, ALU.mult)\
                            .then_inc(at_sm, 1)
                    if 1 <= step < N + 1:
                        s1 = step - 1
                        w = nk(s1 % TT) * P
                        c = (s1 % 4) * 4
                        dve.wait_ge(at_e, a0 + s1 + 1)
                        link(nc.vector.reciprocal(st[:, c + 3:c + 4], st[:, c + 2:c + 3]))
                        nc.vector.tensor_scalar(p[:, s1 % 3, 0:w], p[:, s1 % 3, 0:w], st[:, c + 3:c + 4], None,
                                                ALU.mult).then_inc(at_p, 1)
                    if step >= 2:
                        s2 = step - 2
                        g, t = s2 // TT, s2 % TT
                        dve.wait_ge(at_t, a0 + s2 + 1)
                        k = nk(t)
                        nc.vector.tensor_copy(pT[:, g % 2, 0:k, t * P:(t + 1) * P],
                                              bank(2 + s2 % 2)[:, 0:k * P].rearrange("p (k c) -> p k c", k=k))\
                            .then_inc(at_pT, 1)
                        if t == 2 and g >= 1:
                            lower_out(g - 1)
                lower_out(heads - 1)

            def cross(i):
                split_units(i, "v", KT - 2, 2)
                project(i, "q", KT)
                attend(i, XH, c_p, c_pT, c_stat[:, 8:32], XD ** -0.5, cross_slots, 2, lambda t: MT, None)
                output(i, "out", 1)

            def even(i):
                L = lambda k: e_lam[:, k, :]
                lam = col[:, COLS["lam"]:COLS["lam"] + LRUT]
                dve.wait_ge(e["lam_exp"], 1)
                link(nc.vector.tensor_scalar(L(2), L(1), 2.0, None, ALU.add))
                link(nc.vector.reciprocal(L(3), L(2)))
                link(nc.vector.tensor_tensor(L(2), L(1), L(3), ALU.mult))
                link(nc.vector.tensor_tensor(L(3), L(2), L(2), ALU.mult))
                link(nc.vector.tensor_scalar(L(4), L(3), 1.0 / 19, 1.0 / 17, ALU.mult, ALU.add))
                for d in (15, 13, 11, 9, 7, 5, 3, 1):
                    link(nc.vector.tensor_tensor(L(5), L(4), L(3), ALU.mult))
                    link(nc.vector.tensor_scalar(L(4), L(5), 1.0 / d, None, ALU.add))
                link(nc.vector.scalar_tensor_tensor(L(5), L(4), 2.0, L(2), ALU.mult, ALU.mult))
                link(nc.vector.tensor_scalar(L(4), lam, -1.0, 0.0, ALU.mult, ALU.max))
                link(nc.vector.tensor_tensor(L(5), L(4), L(5), ALU.add))
                nc.vector.tensor_scalar(L(6), L(5), 4.0, None, ALU.mult)
                nc.vector.tensor_scalar(L(7), L(5), -8.0, None, ALU.mult).then_inc(e["lam"], 1)

                project(i, "q_idx", 4)
                project(i, "c_kv", 2)
                split_units(i, "kw_idx", 1)
                dve.wait_ge(e["ssq"], 1)
                nc.vector.tensor_scalar(tmp[:, 2, :], bank(2), 1.0 / RANK, EPS, ALU.mult, ALU.add)\
                    .then_inc(e["ms"], 1)
                dve.wait_ge(e["ms"], 1)
                link(nc.vector.reciprocal(tmp[:, 1, :], tmp[:, 2, :]))
                dve.wait_ge(e["rs"], 1)
                link(nc.vector.tensor_tensor(tmp[:, 2, :], tmp[:, 1, :], tmp[:, 3, :], ALU.mult))
                for k in range(2):
                    c = COLS["kv_norm"] + k
                    nc.vector.scalar_tensor_tensor(e_ck[:, k, :], e_ck[:, k, :], col[:, c:c + 1], tmp[:, 2, :],
                                                   ALU.mult, ALU.mult).then_inc(e["ckn"], 1)
                for k in range(2):
                    dve.wait_ge(e["ck_hi"], k + 1)
                    nc.vector.tensor_tensor(e_ck_lo[:, k, :], e_ck[:, k, :], e_ck_hi[:, k, :].bitcast(f32),
                                            ALU.subtract).then_inc(e["ck_ready"], 1)
                dve.wait_ge(e["wT"], 1)
                nc.vector.tensor_scalar(e_w[:, :, :], bank(3)[:, 0:TT * IH].rearrange("p (t c) -> p t c", t=TT),
                                        IH ** -0.5, ID ** -0.5, ALU.mult, ALU.mult).then_inc(e["w"], 1)
                dve.wait_ge(e["w"], 1)
                for n in range((TT - 1) * IH):
                    b, hd = n // IH, n % IH
                    w = (b + 2) * P
                    dve.wait_ge(e["relu"], n + 1)
                    wh = e_w[:, b + 1, hd:hd + 1]
                    if hd == 0:
                        nc.vector.tensor_scalar(e_sc[:, b, 0:w], tmp[:, n % 2, 0:w], wh, None, ALU.mult)\
                            .then_inc(e["acc"], 1)
                    else:
                        dve.wait_ge(e["acc"], n)
                        nc.vector.scalar_tensor_tensor(e_sc[:, b, 0:w], tmp[:, n % 2, 0:w], wh, e_sc[:, b, 0:w],
                                                       ALU.mult, ALU.add).then_inc(e["acc"], 1)

                def take(r):
                    per = TOPK // 8
                    if r >= (TT - 1) * per:
                        return
                    b = r // per
                    sc = e_sc[:, b, 0:(b + 2) * P]
                    if r % per == 0:
                        dve.wait_ge(e["filled"], b + 1)
                    link(nc.vector.max(e_max8[:, :], sc))
                    link(nc.vector.match_replace(sc, e_max8[:, :], sc, TAKEN))
                    if r % per == per - 1:
                        link(nc.vector.tensor_scalar(sc, sc, TAKEN, NEG, ALU.not_equal, ALU.mult))

                r = 0
                for seg, n in (("x_b", 4), ("uk", 1), ("uv", 1), ("gate", 4), ("q", 4)):
                    for q in range(n):
                        split_units(i, seg, 1, q)
                        for _ in range(4):
                            take(r)
                            r += 1
                for c in range(LRUT):
                    T, R = f_r[:, c, :], tmp[:, c, :]
                    dve.wait_ge(e["tanh"], c + 1)
                    dve.wait_ge(e["sig"], 2 * LRUT)
                    link(nc.vector.tensor_scalar(R, R, 0.5, 0.5, ALU.mult, ALU.add))
                    link(nc.vector.scalar_tensor_tensor(e_p[:, 0, :], T, 1.0, R, ALU.add, ALU.mult))
                    link(nc.vector.tensor_scalar(e_p[:, 0, :], e_p[:, 0, :], -1.0, 2.0, ALU.mult, ALU.add))
                    link(nc.vector.tensor_tensor(R, R, e_p[:, 0, :], ALU.mult))
                    nc.vector.tensor_scalar(e_a[:, c, :], R, 2.0, -1.0, ALU.mult, ALU.add).then_inc(e["bv"], 1)
                for c in range(LRUT):
                    dve.wait_ge(e["sqrt"], c + 1)
                    link(nc.vector.tensor_tensor(e_p[:, 0, :], f_r[:, c, :], tmp[:, c, :], ALU.mult))
                    dve.wait_ge(e["t2"], c + 1)
                    link(nc.vector.tensor_tensor(e_p[:, 0, :], e_p[:, 0, :], e_xc[:, c, :], ALU.mult))
                    dve.wait_ge(e["bv"], LRUT)
                    link(nc.vector.tensor_tensor_scan(e_p[:, 1, :], e_a[:, c, :], e_p[:, 0, :], 0.0,
                                                      ALU.mult, ALU.add))
                    dve.wait_ge(e["gelu"], c + 1)
                    nc.vector.tensor_tensor(e_xc[:, c, :], e_p[:, 1, :], e_gate[:, c, :], ALU.mult)\
                        .then_inc(e["y"], 1)
                for c in range(LRUT):
                    dve.wait_ge(e["y_hi"], c + 1)
                    nc.vector.tensor_tensor(x_lo[:, 4 + c, :], e_xc[:, c, :], x_hi[:, 4 + c, :].bitcast(f32),
                                            ALU.subtract).then_inc(e["y_ready"], 1)
                dve.wait_ge(e["tri"], 1)
                attend(i, AH, e_p, e_pT, e_st, AD ** -0.5, even_slots, 1, lambda t: t + 1,
                       lambda t: e_tri[:, :] if t == 0 else e_sc[:, t - 1, 0:(t + 1) * P])
                output(i, "out", 1)

            def gla(i):
                split_units(i, "g_lr", 1)
                project(i, "q", GH)
                project(i, "k", GH)
                dve.wait_ge(gs["keep"], 2)
                for n in range(GH):
                    z = g_kr[:, n, :]
                    split_units(i, "v", 1, 2 * n)
                    dve.wait_ge(gs["ln"], n + 1)
                    if n > 0:
                        dve.wait_ge(gs["e"], 2 * n)
                    link(nc.vector.scalar_tensor_tensor(tmp[:, 1, :], z, 0.0, tmp[:, 0, :], ALU.min, ALU.subtract))
                    nc.vector.tensor_tensor_scan(tmp[:, 2, :], g_keep[:, :], tmp[:, 1, :], 0.0, ALU.mult, ALU.add)\
                        .then_inc(gs["G"], 1)
                    dve.wait_ge(gs["G"], 2 * n + 1)
                    G = tmp[:, 2, :].rearrange("p (c t) -> p c t", t=CH)
                    nc.vector.tensor_tensor(tmp[:, 3, :].rearrange("p (c t) -> p c t", t=CH),
                                            G[:, :, CH - 1:CH].to_broadcast([P, SEQ // CH, CH]), G, ALU.subtract)\
                        .then_inc(gs["G"], 1)
                    split_units(i, "v", 1, 2 * n + 1)
                    dve.wait_ge(p_free, PT0[i, "k"] + GH + 2)
                    dve.wait_ge(gs["e"], 2 * n + 2)
                    nc.vector.tensor_copy(g_dec[:, n, :],
                                          g_t[:, 0, :].rearrange("p (c t) -> p c t", t=CH)[:, :, CH - 1])
                    nc.vector.scalar_tensor_tensor(g_q[:, n, :], g_q[:, n, :], GDK ** -0.5, g_t[:, 0, :],
                                                   ALU.mult, ALU.mult).then_inc(gs["qk"], 1)
                    nc.vector.tensor_tensor(z, g_k[:, n, :], tmp[:, 3, :], ALU.mult).then_inc(gs["qk"], 1)
                    nc.vector.tensor_tensor(g_k[:, n, :], g_k[:, n, :], g_t[:, 1, :], ALU.mult).then_inc(gs["qk"], 1)
                project(i, "r", KT)
                dve.wait_ge(gs["qk"], 3 * GH)
                dve.wait_ge(gs["zero"], 1)
                dve.wait_ge(gs["mask"], 3)
                for w in range(TT * GH):
                    T, n = w // GH, w % GH
                    dve.wait_ge(gs["att_full"], w + 1)
                    if w >= 2:
                        dve.wait_ge(gs["o_full"], w - 1)
                    nc.vector.copy_predicated(g_att[:, w % 2, :], g_mask[:, :].bitcast(mybir.dt.int32),
                                              bank(w % 2)[:, 0:P]).then_inc(gs["att"], 1)
                    dve.wait_ge(gs["u_full"], w + 1)
                    for a in range(2):
                        c = 2 * T + a
                        if c == SEQ // CH - 1:
                            break
                        new, up = g_S[:, n, (c + 1) % 3, :], bank(2 + 4 * a + w % 2)[:, 0:GDV]
                        if c == 0:
                            ins = nc.vector.tensor_copy(new, up)
                        else:
                            ins = nc.vector.scalar_tensor_tensor(new, g_S[:, n, c % 3, :], g_dec[:, n, c:c + 1], up,
                                                                 ALU.mult, ALU.add)
                        link(ins) if a == 0 and c != SEQ // CH - 2 else ins.then_inc(gs["S"], 1)
                    if w % GH == GH - 1 and T > 0:
                        mean(T - 1)
                mean(TT - 1)
                for T in range(TT):
                    if T == 0:
                        dve.wait_ge(gs["gain_in"], 16)
                    dve.wait_ge(gs["root"], T + 1)
                    at = slice(GH * T, GH * (T + 1))
                    link(nc.vector.tensor_tensor(g_st[:, 2, at], g_st[:, 1, at], g_st[:, 3, at], ALU.mult))
                    for n in range(GH):
                        o = f[:, T, n * GDV:(n + 1) * GDV]
                        nc.vector.scalar_tensor_tensor(o, o, g_st[:, 2, T * GH + n:T * GH + n + 1], g_gain[:, :],
                                                       ALU.mult, ALU.mult).then_inc(gs["on"], 1)
                    if T > 0:
                        gated(i, T - 1)
                gated(i, TT - 1)
                output(i, "out", 1)

            def mean(T):
                dve.wait_ge(gs["osq"], GH * (T + 1))
                inv = g_st[:, 1, GH * T:GH * (T + 1)]
                link(nc.vector.tensor_scalar(inv, g_st[:, 0, GH * T:GH * (T + 1)], 1.0 / GDV, EPS, ALU.mult, ALU.add))
                link(nc.vector.reciprocal(inv, inv))

            def gated(i, T):
                if T >= 2:
                    dve.wait_ge(gs["y_ready"], 2 * (T - 1))
                for b in range(2):
                    dve.wait_ge(gs["oT"], 2 * T + b + 1)
                    if T == 0 and b == 0:
                        dve.wait_ge(p_free, PT0[i, "r"] + KT + 2)
                    y = tmp[:, 2 * (T % 2) + b, :].rearrange("p (k c) -> p k c", k=4)
                    nc.vector.tensor_tensor(y, bank(2 * (T % 2) + b).rearrange("p (k c) -> p k c", k=4),
                                            g_r[:, 4 * b:4 * b + 4, T * P:(T + 1) * P], ALU.mult).then_inc(gs["y"], 1)
                for b in range(2):
                    dve.wait_ge(gs["y_hi"], 2 * T + b + 1)
                    y = tmp[:, 2 * (T % 2) + b, :].rearrange("p (k c) -> p k c", k=4)
                    nc.vector.tensor_tensor(x_lo[:, 4 * b:4 * b + 4, T * P:(T + 1) * P], y,
                                            x_hi[:, 4 * b:4 * b + 4, T * P:(T + 1) * P].bitcast(f32),
                                            ALU.subtract).then_inc(gs["y_ready"], 1)

            for i in range(NP + 1):
                norm(i)
                if i < NP:
                    if parts[i][0] == "ffn":
                        ffn(i)
                    elif parts[i][0] == "cross":
                        cross(i)
                    elif parts[i][0] == "even":
                        even(i)
                    else:
                        gla(i)

        @block.tensor
        def _(pe):
            pe.sem_inc(w_free, 2)
            pe.sem_inc(oT_full, 2)
            pe.wait_ge(consts, 5)

            def turn_x(i, t):
                pe.wait_ge(xs_ready, TT * i + t + 1)
                if t >= 2:
                    pe.wait_ge(x_ready, 2 * TT * i + 2 * (t - 2) + 2)
                for b in range(2):
                    for k in range(4):
                        last = nc.tensor.transpose(bank(4 + 2 * (t % 2) + b)[:, k * P:(k + 1) * P],
                                                   f[:, t, (4 * b + k) * P:(4 * b + k + 1) * P], ident[:, :])
                    last.then_inc(xT_ready, 1)

            def norm(i, b0):
                u0, h0 = U[i, UNITS[parts[i][0]][0][0]], SEQ // 2

                def half_unit(q, hf):
                    u = u0 + q
                    pe.wait_ge(w_ready, u + 1)
                    return unit_blocks(u % 2, bank(b0[q])[:, hf * h0:(hf + 1) * h0], slice(hf * h0, (hf + 1) * h0))

                for t in range(TT - 1):
                    turn_x(i, t)
                if i == 0:
                    turn_x(i, TT - 1)
                pe.wait_ge(x_ready, 2 * TT * i + TT)
                half_unit(0, 0)
                if i > 0:
                    turn_x(i, TT - 1)
                half_unit(1, 0)
                pe.wait_ge(x_ready, 2 * TT * (i + 1))
                for q in range(2):
                    half_unit(q, 1).then_inc(w_free, 1)

            def unit_blocks(s, dst, cols_of_x):
                for b in range(UB):
                    last = three(dst, w_hi[:, s, b * P:(b + 1) * P], w_lo[:, s, b * P:(b + 1) * P],
                                 x_hi[:, b, cols_of_x], x_lo[:, b, cols_of_x], b == 0, b == UB - 1)
                return last

            def ffn(i):
                n0, u0 = nffn[i] * FT, U[i, "gate_up"]
                pe.wait_ge(gu_free, n0 + 1)
                norm(i, (0, 1))

                def pair(j, jj):
                    pe.wait_ge(gu_free, j + (n0 + 1))
                    unit_tile(pe, 2 * j + u0, u0 % 2, bank(2 * jj), x_hi, x_lo)
                    unit_tile(pe, 2 * j + (u0 + 1), (u0 + 1) % 2, bank(2 * jj + 1), x_hi, x_lo)

                pair(1, 1)
                with pe.Fori(1, FT // 2) as it:
                    pair(2 * it, 0)
                    pair(2 * it + 1, 1)
                output(i, "down", DU, act_hi, act_lo, FT, lambda q: pe.wait_ge(act_ready, n0 + min(FT, UB * (q + 1)) + 2))

            def output(i, seg, per, src_hi, src_lo, nk, ready=None):
                u0 = U[i, seg]

                def tile(n, s0, kk, between):
                    pe.wait_ge(o_free, n + (KT * i + 1))
                    for q in range(per):
                        if ready is not None and between is None:
                            ready(q)
                        kb = min(UB, nk - q * UB)
                        unit_tile(pe, n * per + (u0 + q), (s0 + q) % 2, bank(4 + kk), src_hi, src_lo, q * UB, kb,
                                  q == 0, q == per - 1, between if q == 0 else None)

                def turn(n, kk):
                    pe.wait_ge(o_free, n + (KT * i + 3))
                    pe.wait_ge(f_ready, n + (KT * i + 1))
                    for t in range(TT):
                        nc.tensor.transpose(bank(6)[:, t * P:(t + 1) * P], tmp[:, kk, t * P:(t + 1) * P], ident[:, :])
                    for t in range(TT):
                        dst = bank(7)[:, n * TT + t:n * TT + t + 1] if isinstance(n, int) \
                            else bank(7)[:, bass.ds(n * TT + t, 1)]
                        last = nc.tensor.matmul(dst, tmp[:, 2 + kk, t * P:(t + 1) * P], ones[:, 0:1],
                                                start=True, stop=True)
                    last.then_inc(oT_full, 1)

                tile(0, u0 % 2, 0, None)
                mem_next = i + 1 < NP and parts[i + 1][0] == "cross"
                for first, end in ((0, 1), (1, KT // 2 - 1)) if mem_next else ((0, KT // 2 - 1),):
                    with pe.Fori(first, end) as it:
                        tile(2 * it + 1, (u0 + per) % 2, 1, lambda: turn(2 * it, 0))
                        tile(2 * it + 2, u0 % 2, 0, lambda: turn(2 * it + 1, 1))
                if mem_next:
                    mem_turn(i)
                tile(KT - 1, (u0 + per * (KT - 1)) % 2, 1, lambda: turn(KT - 2, 0))
                turn(KT - 1, 1)

            def project_tile(i, seg, j, jj, xh, xl, w=SEQ):
                u0, t0 = U[i, seg], PT0[i, seg]
                pe.wait_ge(p_free, j + (t0 + 1))
                unit_tile(pe, j + u0, (u0 + jj) % 2, bank((t0 + jj) % 2)[:, 0:w], xh, xl)

            def project(i, seg, n, xh, xl, w=SEQ, done=0):
                if done % 2:
                    project_tile(i, seg, done, 1, xh, xl, w)
                with pe.Fori((done + 1) // 2, n // 2) as it:
                    for jj in range(2):
                        project_tile(i, seg, 2 * it + jj, jj, xh, xl, w)

            def values(i, seg, group, units, off, xh, xl, tiles, b0):
                for q in range(units):
                    v = U[i, seg] + off + q
                    pe.wait_ge(w_ready, v + 1)
                    for j in range(2):
                        wh, wl = (w[:, v % 2, j * SEQ:(j + 1) * SEQ] for w in (w_hi, w_lo))
                        k = 2 * q + j
                        for t in range(tiles):
                            ah, al = (a[:, k, t * P:(t + 1) * P] for a in (xh, xl))
                            dst = bank(b0 + t)
                            first, final = k == 0, k == 2 * units - 1
                            nc.tensor.matmul(dst, ah, wh, start=first, stop=False)
                            nc.tensor.matmul(dst, ah, wl, start=False, stop=False)
                            last = nc.tensor.matmul(dst, al, wh, start=False, stop=final)
                    last.then_inc(w_free, 1)

            def attend(i, heads, p, pT, nk, scores, mix, direct):
                a0 = A0[i]
                N = heads * TT
                for step in range(N + 4):
                    if step < N:
                        if step >= 2:
                            pe.wait_ge(at_e if direct else at_sm, a0 + step - 1)
                        scores(step // TT, step % TT, bank(step % 2)).then_inc(at_s, 1)
                    if 2 <= step < N + 2:
                        s2 = step - 2
                        pe.wait_ge(at_p, a0 + s2 + 1)
                        if s2 >= 2:
                            pe.wait_ge(at_pT, a0 + s2 - 1)
                        for k in range(nk(s2 % TT)):
                            last = nc.tensor.transpose(bank(2 + s2 % 2)[:, k * P:(k + 1) * P],
                                                       p[:, s2 % 3, k * P:(k + 1) * P], ident[:, :])
                        last.then_inc(at_t, 1)
                    if step >= 3 and (step - 3) % TT == TT - 1:
                        g = (step - 3) // TT
                        pe.wait_ge(at_pT, a0 + TT * (g + 1))
                        mix(g)

            def mem_turn(i):
                c = ncross[i + 1]
                for m in range(MT):
                    pe.wait_ge(mem_n, MT * c + m + 1)
                    for b in range(2):
                        for k in range(4):
                            last = nc.tensor.transpose(bank(2 * m + b)[:, k * P:(k + 1) * P],
                                                       c_mem[:, m, (4 * b + k) * P:(4 * b + k + 1) * P], ident[:, :])
                        last.then_inc(memT_ready, 1)

            def cross(i):
                c = ncross[i]
                pe.wait_ge(memT_used, 4 * (c + 1))
                for k in range(KT):
                    project_tile(i, "k", k, k % 2, c_mem_hi, c_mem_lo, NMEM)
                    if k in (2, 5, 7):
                        turn_x(i, {2: 0, 5: 1, 7: 2}[k])
                values(i, "v", 0, 4, 0, c_mem_hi, c_mem_lo, MT, 2)
                turn_x(i, TT - 1)
                pe.wait_ge(p_free, PT0[i, "k"] + KT + 2)
                values(i, "v", 1, 4, 4, c_mem_hi, c_mem_lo, MT, 0)
                pe.wait_ge(x_ready, 2 * TT * (i + 1))
                pe.wait_ge(v_ready, V0[i] + 2)
                project(i, "q", KT, x_hi, x_lo)
                pe.wait_ge(p_free, PT0[i, "q"] + KT + 2)
                pe.wait_ge(v_ready, V0[i] + 2)

                def scores(g, t, dst):
                    for j in range(2):
                        last = nc.tensor.matmul(dst[:, 0:NMEM], c_qT[:, 2 * g + j, t * P:(t + 1) * P],
                                                c_kT[:, 2 * g + j, :], start=j == 0, stop=j == 1)
                    return last

                def mix(g):
                    if g > 0:
                        pe.wait_ge(at_olo, O0[i] + 2 * g)
                    for o in range(2):
                        for m in range(MT):
                            last = nc.tensor.matmul(bank(4 + o), c_v[:, m, g * XD + o * P:g * XD + (o + 1) * P],
                                                    c_pT[:, g % 2, m, :], start=m == 0, stop=m == MT - 1)
                        last.then_inc(at_o, 1)

                attend(i, XH, c_p, c_pT, lambda t: MT, scores, mix, True)
                pe.wait_ge(at_olo, O0[i] + 2 * XH)
                output(i, "out", 1, x_hi, x_lo, KT)

            def one_tile(i, seg):
                pe.wait_ge(p_free, PT0[i, seg] + 1)
                u = U[i, seg]
                unit_tile(pe, u, u % 2, bank(PT0[i, seg] % 2), x_hi, x_lo)

            def even(i):
                t0 = PT0[i, "q_idx"]
                pe.wait_ge(p_free, t0 + 2)
                norm(i, (t0 % 2, 1 - t0 % 2))
                project(i, "q_idx", 4, x_hi, x_lo, done=2)
                project(i, "c_kv", 2, x_hi, x_lo)
                one_tile(i, "kw_idx")
                for k in range(2):
                    pe.wait_ge(e["sq"], k + 1)
                    last = nc.tensor.matmul(bank(2), ones[:, :], tmp[:, k, :], start=k == 0, stop=k == 1)
                last.then_inc(e["ssq"], 1)
                pe.wait_ge(p_free, PT0[i, "kw_idx"] + 3)
                for t in range(TT):
                    last = nc.tensor.transpose(bank(3)[:, t * IH:(t + 1) * IH], e_wi[:, t * P:(t + 1) * P],
                                               ident[0:IH, 0:IH])
                last.then_inc(e["wT"], 1)
                pe.wait_ge(e["ms"], 1)
                pe.wait_ge(e["w"], 1)
                for n in range((TT - 1) * IH):
                    b, hd = n // IH + 1, n % IH
                    p0 = hd % 2 * ID
                    if n >= 2:
                        pe.wait_ge(e["relu"], n - 1)
                    nc.tensor.matmul(bank(2 + n % 2)[:, 0:(b + 1) * P], e_qi[p0:p0 + ID, hd // 2, b * P:(b + 1) * P],
                                     e_k2[p0:p0 + ID, 0:(b + 1) * P], start=True, stop=True).then_inc(e["s"], 1)
                project(i, "x_b", 4, x_hi, x_lo)
                pe.wait_ge(e["ck_ready"], 2)
                u = U[i, "uk"]
                pe.wait_ge(w_ready, u + 1)
                for n in range(4):
                    pe.wait_ge(p_free, PT0[i, "uk"] + n + 1)
                    for k in range(2):
                        c = (2 * n + k) * P
                        last = three(bank((PT0[i, "uk"] + n) % 2), w_hi[:, u % 2, c:c + P], w_lo[:, u % 2, c:c + P],
                                     e_ck_hi[:, k, :], e_ck_lo[:, k, :], k == 0, k == 1)
                    last.then_inc(e["uk_full"] if n < 3 else w_free, 1)
                values(i, "uv", 0, 1, 0, e_ck_hi, e_ck_lo, TT, 4)
                project(i, "gate", 4, x_hi, x_lo)
                project(i, "q", 4, x_hi, x_lo)
                pe.wait_ge(e["bd"], 64)
                pe.wait_ge(v_ready, V0[i] + 1)
                for n in range(2):
                    if n == 1:
                        pe.wait_ge(p_free, PT0[i, "q"] + 4 + 2)
                        pe.wait_ge(e["relu"], (TT - 1) * IH)
                    for c in range(LRUT):
                        if n == 0:
                            pe.wait_ge(e["conv"], c + 1)
                        nc.tensor.matmul(bank(4 * (1 - n) + c), e_bd[:, n, c, :], e_xc[:, c, :], start=True, stop=True)\
                            .then_inc(e["gates"], 1)
                pe.wait_ge(e["sig"], 2 * LRUT)

                def scores(g, t, dst):
                    p0, w = g % 2 * AD, (t + 1) * P
                    return nc.tensor.matmul(dst[:, 0:w], e_qT[p0:p0 + AD, g // 2, t * P:(t + 1) * P],
                                            e_kT[p0:p0 + AD, g // 2, 0:w], start=True, stop=True)

                def mix(g):
                    p0, j = g % 2 * AD, g // 2
                    if g % 2 == 0 and j >= 2:
                        pe.wait_ge(at_olo, O0[i] + j - 1)
                    for k in range(TT):
                        last = nc.tensor.matmul(bank(4 + j % 2)[p0:p0 + AD, k * P:SEQ], e_v[:, k, g * AD:(g + 1) * AD],
                                                e_pT[:, g % 2, k, k * P:SEQ], start=k == 0, stop=k == TT - 1)
                    if g % 2:
                        last.then_inc(at_o, 1)

                attend(i, AH, e_p, e_pT, lambda t: t + 1, scores, mix, False)
                pe.wait_ge(at_olo, O0[i] + AH // 2)
                pe.wait_ge(e["y_ready"], LRUT)
                output(i, "out", 1, x_hi, x_lo, KT)

            def gla(i):
                t0 = PT0[i, "g_lr"]
                pe.wait_ge(p_free, t0 + 2)
                norm(i, (t0 % 2, 1 - t0 % 2))
                project(i, "q", GH, x_hi, x_lo, done=1)
                pe.wait_ge(gs["w2_in"], 16)
                for n in range(GH):
                    nc.tensor.matmul(bank(4 + n), g_w2[:, n * GDK:(n + 1) * GDK], g_lr[:, :], start=True, stop=True)\
                        .then_inc(gs["z_full"], 1)
                project(i, "k", GH, x_hi, x_lo)
                pe.wait_ge(gs["z"], GH)
                values(i, "v", 0, 4, 0, x_hi, x_lo, TT, 4)
                pe.wait_ge(p_free, PT0[i, "k"] + GH + 2)
                values(i, "v", 1, 4, 4, x_hi, x_lo, TT, 0)
                pe.wait_ge(v_ready, V0[i] + 2)
                for n in range(GH):
                    pe.wait_ge(gs["qk"], 3 * n + 2)
                    for t in range(TT):
                        last = nc.tensor.transpose(bank(4 + n)[:, t * P:(t + 1) * P], g_kr[:, n, t * P:(t + 1) * P],
                                                   ident[:, :])
                    last.then_inc(gs["krT"], 1)
                project(i, "r", KT, x_hi, x_lo)
                pe.wait_ge(gs["krt"], GH)
                pe.wait_ge(p_free, PT0[i, "r"] + KT + 2)
                pe.wait_ge(gs["qk"], 3 * GH)

                def mixed(w):
                    T, n = w // GH, w % GH
                    pe.wait_ge(gs["att"], w + 1)
                    pe.wait_ge(gs["S"], w + 1)
                    if w >= 2:
                        pe.wait_ge(gs["osq"], w - 1)
                    dst = bank(4 + w % 2)
                    nc.tensor.matmul(dst[:, 0:GDV], g_att[:, w % 2, :], g_v[:, T, n * GDV:(n + 1) * GDV],
                                     start=True, stop=False, skip_group_check=True)
                    for a in range(2):
                        c = 2 * T + a
                        if c == 0:
                            continue
                        last = nc.tensor.matmul(dst[a * CH:(a + 1) * CH, 0:GDV], g_q[:, n, c * CH:(c + 1) * CH],
                                                g_S[:, n, c % 3, :], start=False, stop=a == 1, skip_group_check=True)
                    last.then_inc(gs["o_full"], 1)

                for w in range(TT * GH + 1):
                    if w < TT * GH:
                        T, n = w // GH, w % GH
                        if w >= 2:
                            pe.wait_ge(gs["att"], w - 1)
                        nc.tensor.matmul(bank(w % 2)[:, 0:P], g_k[:, n, T * P:(T + 1) * P], g_q[:, n, T * P:(T + 1) * P],
                                         start=True, stop=True).then_inc(gs["att_full"], 1)
                        if w >= 2:
                            pe.wait_ge(gs["S"], w - 1)
                        for a in range(2):
                            rows = slice(a * CH, (a + 1) * CH)
                            last = nc.tensor.matmul(bank(2 + 4 * a + w % 2)[:, 0:GDV], g_krt[rows, T, n, :],
                                                    g_v[rows, T, n * GDV:(n + 1) * GDV], start=True, stop=True)
                        last.then_inc(gs["u_full"], 1)
                    if w >= 1:
                        mixed(w - 1)
                for T in range(TT):
                    pe.wait_ge(gs["on"], GH * (T + 1))
                    if T >= 2:
                        pe.wait_ge(gs["y"], 2 * (T - 1))
                    for b in range(2):
                        for k in range(4):
                            last = nc.tensor.transpose(bank(2 * (T % 2) + b)[:, k * P:(k + 1) * P],
                                                       f[:, T, (4 * b + k) * P:(4 * b + k + 1) * P], ident[:, :])
                        last.then_inc(gs["oT"], 1)
                pe.wait_ge(gs["y_ready"], 2 * TT)
                output(i, "out", 1, x_hi, x_lo, KT)

            for i in range(NP):
                if parts[i][0] == "ffn":
                    ffn(i)
                elif parts[i][0] == "cross":
                    cross(i)
                elif parts[i][0] == "even":
                    even(i)
                else:
                    gla(i)


def square_units(w):
    K, N = w.shape
    kb = -(-K // UW) * UB
    padded = np.zeros((kb * P, N), w.dtype)
    padded[:K] = w
    return padded.reshape(kb // UB, UB, P, N // P, P).transpose(3, 0, 2, 1, 4).reshape(-1, P, UW)


def padded_columns(w, n):
    out = np.zeros((w.shape[0], n), w.dtype)
    out[:, :w.shape[1]] = w
    return out


def row_units(w):
    K, N = w.shape
    return w.reshape(K // (2 * P), 2, P, N // 512, 512).transpose(3, 0, 2, 1, 4).reshape(-1, P, UW)


def weight_stream(a, parts):
    units = []
    for kind, l, k in parts:
        if kind == "ffn":
            gu = square_units(a["ffn_w_gu"][l, k])
            units.append(gu.reshape(2, FT, P, UW).transpose(1, 0, 2, 3).reshape(-1, P, UW))
            units.append(square_units(a["ffn_w_down"][l, k]))
        elif kind == "cross":
            kv = a["xa_w_kv"][l]
            units += [square_units(kv[:, :DM]), row_units(kv[:, DM:]), square_units(a["xa_w_q"][l]),
                      square_units(a["xa_w_o"][l])]
        elif kind == "even":
            e = l // 2
            w = a["ev_w_in"][e]
            q, ckv, qi, ki, wi, gate, xb = np.split(w, np.cumsum([512, RANK, IH * ID, ID, IH, 512]), axis=1)
            units += [square_units(qi), square_units(ckv),
                      square_units(padded_columns(np.concatenate([ki, wi], 1), P)), square_units(xb)]
            uk = a["ev_w_uk"][e].reshape(2, P, 4, P).transpose(1, 2, 0, 3).reshape(1, P, UW)
            units += [uk, row_units(a["ev_w_uv"][e]), square_units(gate), square_units(q),
                      square_units(a["ev_w_out"][e])]
        else:
            o = l // 2
            q, k_, v, g, r = np.split(a["od_w_in"][o], np.cumsum([512, 512, DM, GR]), axis=1)
            units += [square_units(padded_columns(g, P)), square_units(q), square_units(k_), row_units(v),
                      square_units(r), square_units(a["od_w_out"][o])]
    return np.ascontiguousarray(np.concatenate(units))


def arrays_for(a, parts):
    a = {k: np.asarray(v) for k, v in a.items()}
    norms = a["norms"]
    pre = {"ffn": (0, 7), "even": (2, 2), "gla": (2, 2), "cross": (4, 4)}
    post = {"ffn": (1, 8), "even": (3, 3), "gla": (3, 3), "cross": (5, 5)}

    def column(v):
        return v.reshape(-1, P).T

    cols = [column(a["ev_kv_norm"][0])]
    cols += [a["ev_conv_w"][0].reshape(CONV, LRUT, P).transpose(2, 1, 0).reshape(P, -1)]
    cols += [column(a[n][0]) for n in ("ev_conv_b", "ev_b_ra", "ev_b_ri", "ev_lam", "od_b_g")]
    cols += [column(norms[l, post[kind][k]]) for kind, l, k in parts]
    return {
        "x": a["x"][0], "mem": a["mem"][0], "wstream": weight_stream(a, parts),
        "cols": np.ascontiguousarray(np.concatenate(cols, 1)),
        "gains": np.stack([norms[l, pre[kind][k]] for kind, l, k in parts]),
        "mem_gains": np.ascontiguousarray(norms[:, 6]),
        "head_gain": a["od_head_norm"][:1],
        "w_ra": a["ev_w_ra"][0], "w_ri": a["ev_w_ri"][0], "w_g2": a["od_w_g2"][0],
    }


def kernel(**inputs):
    import concourse.bacc as _bacc
    from concourse.bass_utils import run_bass_kernel_spmd as _run

    nc = _bacc.Bacc("TRN2", target_bir_lowering=False, num_devices=1)
    arrays = {f"in_{k}": np.ascontiguousarray(v) for k, v in arrays_for(inputs, PARTS).items()}
    args = [nc.dram_tensor(k, v.shape, mybir.dt.from_np(v.dtype), kind="ExternalInput").ap() for k, v in arrays.items()]
    out = nc.dram_tensor("out_0_dram", (SEQ, DM), mybir.dt.float32, kind="ExternalOutput").ap()
    trunk(nc, PARTS, *args, out)
    r = _run(nc, [arrays], core_ids=[0])
    return r.results[0]["out_0_dram"].reshape(1, SEQ, DM)
```

```python
import numpy as np
import concourse.bass as bass
from concourse import mybir
from contextlib import ExitStack

DM, SEQ, NMEM = 1024, 512, 256
DFF = 2816
P = 128
KT = DM // P
TT = SEQ // P
FT = DFF // P
MT = NMEM // P
EPS = 1e-6
UB = 8
UW = UB * P
XH, XD = 4, 256
AH, AD = 8, 64
IH, ID = 8, 64
TOPK = min(256, SEQ // 4)
RANK = 256
LRUT = 512 // P
CONV = 4
GH, GDK, GDV = 4, 128, 256
CH = 64
GR = 16

PARTS = [("ffn", 0, 0), ("even", 0, 0), ("cross", 0, 0), ("ffn", 0, 1),
         ("ffn", 1, 0), ("gla", 1, 0), ("cross", 1, 0), ("ffn", 1, 1)]
UNITS = {
    "ffn": [("gate_up", 2 * FT), ("down", FT)],
    "even": [("q_idx", 4), ("c_kv", 2), ("kw_idx", 1), ("x_b", 4), ("uk", 1), ("uv", 1), ("gate", 4), ("q", 4),
             ("out", KT)],
    "cross": [("k", KT), ("v", KT), ("q", KT), ("out", KT)],
    "gla": [("g_lr", 1), ("q", 4), ("k", 4), ("v", KT), ("r", KT), ("out", KT)],
}
COLS = {}
_n = 0
for _name, _w in [("kv_norm", RANK // P), ("conv_w", LRUT * CONV), ("conv_b", LRUT),
                  ("b_ra", LRUT), ("b_ri", LRUT), ("lam", LRUT), ("b_g", GH)]:
    COLS[_name] = _n
    _n += _w


def unit_starts(parts):
    at, n = {}, 0
    for i, (kind, _, _) in enumerate(parts):
        for seg, k in UNITS[kind]:
            at[i, seg] = n
            n += k
    return at, n


def trunk(nc, parts, x, mem, wstream, cols, gains, post_gains, mem_gains, head_gain, w_ra, w_ri, w_g2, out):
    f32, f32r = mybir.dt.float32, mybir.dt.float32r
    ALU, ACT, AX = mybir.AluOpType, mybir.ActivationFunctionType, mybir.AxisListType
    U, _ = unit_starts(parts)
    NU = wstream.shape[0]
    NP = len(parts)

    ctx = ExitStack()
    with ctx:
        def sb(name, shape, dt=f32):
            return ctx.enter_context(nc.sbuf_tensor(name, shape, dt))

        def sem(name):
            return ctx.enter_context(nc.semaphore(name))

        h = sb("h", [P, TT, DM])
        f = sb("f", [P, TT, DM])
        x_hi = sb("x_hi", [P, KT, SEQ], f32r)
        x_lo = sb("x_lo", [P, KT, SEQ], f32r)
        w_raw = sb("w_raw", [P, 2, UW])
        w_hi = sb("w_hi", [P, 2, UW], f32r)
        w_lo = sb("w_lo", [P, 2, UW], f32r)
        tmp = sb("tmp", [P, 4, SEQ])
        gain_bc = sb("gain_bc", [P, DM])
        col = sb("col", [P, cols.shape[1]])
        ident = sb("ident", [P, P])
        ones = sb("ones", [P, P])
        eps = sb("eps", [P, 2])
        stat = sb("stat", [P, NP + 1, 32])
        with ExitStack() as own:
            def part_sb(name, shape, dt=f32):
                return own.enter_context(nc.sbuf_tensor(name, shape, dt))
            act_hi = part_sb("act_hi", [P, FT, SEQ], f32r)
            act_lo = part_sb("act_lo", [P, FT, SEQ], f32r)
        with ExitStack() as own:
            def part_sb(name, shape, dt=f32):
                return own.enter_context(nc.sbuf_tensor(name, shape, dt))
            c_mem = part_sb("c_mem", [P, MT, DM])
            c_gain = part_sb("c_gain", [P, DM])
            c_mem_hi = part_sb("c_mem_hi", [P, KT, NMEM], f32r)
            c_mem_lo = part_sb("c_mem_lo", [P, KT, NMEM], f32r)
            c_kT = part_sb("c_kT", [P, KT, NMEM])
            c_v = part_sb("c_v", [P, MT, DM])
            c_qT = part_sb("c_qT", [P, KT, SEQ])
            c_p = part_sb("c_p", [P, 3, NMEM])
            c_pT = part_sb("c_pT", [P, 2, MT, SEQ])
            c_stat = part_sb("c_stat", [P, 80])
        with ExitStack() as own:
            def part_sb(name, shape, dt=f32):
                return own.enter_context(nc.sbuf_tensor(name, shape, dt))
            e_k2 = part_sb("e_k2", [P, SEQ])
            e_wi = part_sb("e_wi", [IH, SEQ])
            e_w = part_sb("e_w", [P, TT, IH])
            e_kT = part_sb("e_kT", [P, 4, SEQ])
            e_v = part_sb("e_v", [P, TT, AH * AD])
            e_xc = part_sb("e_xc", [P, LRUT, SEQ])
            e_gate = part_sb("e_gate", [P, LRUT, SEQ])
            e_qT = part_sb("e_qT", [P, 4, SEQ])
            e_sc = part_sb("e_sc", [P, TT - 1, SEQ])
            e_tri = part_sb("e_tri", [P, P])
            e_bd = part_sb("e_bd", [P, 2, LRUT, P])
            e_max8 = part_sb("e_max8", [P, 8])
            e_lam = part_sb("e_lam", [P, 8, LRUT])
            e_st = part_sb("e_st", [P, 16])
            e_t = part_sb("e_t", [P, 2, SEQ])
            with ExitStack() as early:
                e_qi = early.enter_context(nc.sbuf_tensor("e_qi", [P, 4, SEQ], f32))
                e_ck = early.enter_context(nc.sbuf_tensor("e_ck", [P, 2, SEQ], f32))
                e_ck_hi = early.enter_context(nc.sbuf_tensor("e_ck_hi", [P, 2, SEQ], f32r))
                e_ck_lo = early.enter_context(nc.sbuf_tensor("e_ck_lo", [P, 2, SEQ], f32r))
                e_xb = early.enter_context(nc.sbuf_tensor("e_xb", [P, LRUT, SEQ + 4], f32))
            e_p = part_sb("e_p", [P, 3, SEQ])
            e_pT = part_sb("e_pT", [P, 2, TT, SEQ])
        with ExitStack() as own:
            def part_sb(name, shape, dt=f32):
                return own.enter_context(nc.sbuf_tensor(name, shape, dt))
            g_q = part_sb("g_q", [P, GH, SEQ])
            g_k = part_sb("g_k", [P, GH, SEQ])
            g_kr = part_sb("g_kr", [P, GH, SEQ])
            g_krt = part_sb("g_krt", [P, TT, GH, P])
            g_v = part_sb("g_v", [P, TT, DM])
            g_r = part_sb("g_r", [P, KT, SEQ])
            g_lr = part_sb("g_lr", [GR, SEQ])
            g_w2 = part_sb("g_w2", [GR, GH * GDK])
            g_t = part_sb("g_t", [P, 2, SEQ])
            g_S = part_sb("g_S", [P, GH, 3, GDV])
            g_dec = part_sb("g_dec", [P, GH, SEQ // CH])
            g_att = part_sb("g_att", [P, 2, P])
            g_mask = part_sb("g_mask", [P, P])
            g_gain = part_sb("g_gain", [P, GDV])
            g_st = part_sb("g_st", [P, 4, TT * GH])
            g_keep = part_sb("g_keep", [P, SEQ])
        ps = ctx.enter_context(nc.psum_tensor("ps", [P, 8, SEQ], f32))

        def bank(b):
            return ps[:, b, :]

        w_in = [sem("w_in0"), sem("w_in1")]
        w_hi_ready = sem("w_hi_ready")
        w_ready = sem("w_ready")
        w_free = sem("w_free")
        cols_in = sem("cols_in")
        x_in = [sem(f"x_in{t}") for t in range(TT)]
        gain_in = sem("gain_in")
        consts = sem("consts")
        ssq_ready = sem("ssq_ready")
        root_ready = sem("root_ready")
        h_ready = sem("h_ready")
        h_sq = sem("h_sq")
        xs_ready = sem("xs_ready")
        xT_ready = sem("xT_ready")
        x_hi_ready = sem("x_hi_ready")
        x_ready = sem("x_ready")
        stat_link = sem("stat_link")
        gu_free = sem("gu_free")
        silu_ready = sem("silu_ready")
        act_hi_ready = sem("act_hi_ready")
        act_ready = sem("act_ready")
        o_full = sem("o_full")
        o_sq = sem("o_sq")
        f_ready = sem("f_ready")
        post_in = sem("post_in")
        p_free = sem("p_free")
        v_ready = sem("v_ready")
        mem_in = sem("mem_in")
        mem_sq = sem("mem_sq")
        mem_root = sem("mem_root")
        mem_n = sem("mem_n")
        memT_ready = sem("memT_ready")
        memT_hi = sem("memT_hi")
        memT_used = sem("memT_used")
        at_s = sem("at_s")
        at_sm = sem("at_sm")
        at_e = sem("at_e")
        at_p = sem("at_p")
        at_t = sem("at_t")
        at_pT = sem("at_pT")
        at_o = sem("at_o")
        at_ohi = sem("at_ohi")
        at_olo = sem("at_olo")
        out_done = sem("out_done")
        e_names = ["sq", "ssq", "ms", "rs", "ckn", "ck_hi", "ck_ready", "wT", "w", "s", "relu", "acc", "filled",
                   "uk_full", "tri", "bd0", "bd", "pad", "conv", "gates", "sig", "bv", "tanh", "exp", "sqrt",
                   "gelu", "t2", "y", "y_hi", "y_ready", "lam", "lam_abs", "lam_exp", "pool_link"]
        e = {n: sem("e_" + n) for n in e_names}
        g_names = ["z_full", "z", "abs", "exp", "ln", "G", "e", "qk", "krT", "krt", "att_full", "att", "u_full",
                   "S", "o_full", "osq", "root", "on", "oT", "y", "y_hi", "y_ready", "w2_in", "gain_in",
                   "mask", "keep", "zero"]
        gs = {n: sem("g_" + n) for n in g_names}

        block = ctx.enter_context(nc.Block())

        nffn = [sum(k == "ffn" for k, _, _ in parts[:i]) for i in range(NP)]
        ncross = [sum(k == "cross" for k, _, _ in parts[:i]) for i in range(NP)]
        PROJ = {"ffn": {}, "cross": {"k": KT, "q": KT},
                "even": {"q_idx": 4, "c_kv": 2, "kw_idx": 1, "x_b": 4, "uk": 4, "gate": 4, "q": 4},
                "gla": {"g_lr": 1, "q": 4, "k": 4, "r": KT}}
        PT0, n = {}, 0
        for i, (kind, _, _) in enumerate(parts):
            for seg, k in PROJ[kind].items():
                PT0[i, seg] = n
                n += k
        VG = {"ffn": 0, "cross": 2, "even": 1, "gla": 2}
        V0 = [sum(VG[k] for k, _, _ in parts[:i]) for i in range(NP)]
        ATI = {"ffn": 0, "cross": XH * TT, "even": AH * TT, "gla": 0}
        ATO = {"ffn": 0, "cross": XH * 2, "even": AH // 2, "gla": 0}
        A0 = [sum(ATI[k] for k, _, _ in parts[:i]) for i in range(NP)]
        O0 = [sum(ATO[k] for k, _, _ in parts[:i]) for i in range(NP)]

        def split_hi(act, v, s):
            act.wait_ge(w_in[s], (v // 2 + 1) * 16 if isinstance(v, int) else v * 8 + (16 if s == 0 else 8))
            act.wait_ge(w_free, v + 1)
            nc.scalar.activation(w_hi[:, s, :], w_raw[:, s, :], ACT.Copy).then_inc(w_hi_ready, 1)

        def split_lo(dve, v, s):
            dve.wait_ge(w_hi_ready, v + 1)
            nc.vector.tensor_tensor(w_lo[:, s, :], w_raw[:, s, :], w_hi[:, s, :].bitcast(f32), ALU.subtract)\
                .then_inc(w_ready, 1)

        def three(dst, wh, wl, xh, xl, start, stop):
            nc.tensor.matmul(dst, wh, xh, start=start, stop=False)
            nc.tensor.matmul(dst, wh, xl, start=False, stop=False)
            return nc.tensor.matmul(dst, wl, xh, start=False, stop=stop)

        def unit_tile(pe, v, s, dst, xh, xl):
            pe.wait_ge(w_ready, v + 1)
            for b in range(UB):
                last = three(dst, w_hi[:, s, b * P:(b + 1) * P], w_lo[:, s, b * P:(b + 1) * P],
                             xh[:, b, :], xl[:, b, :], b == 0, b == UB - 1)
            last.then_inc(w_free, 1)
            return last

        f_r = f[:, 0:2, :].rearrange("p a (b c) -> p (a b) c", c=SEQ)
        f_i = f[:, 2:4, :].rearrange("p a (b c) -> p (a b) c", c=SEQ)
        gate_bank = (4, 5, 6, 7, 2, 3, 4, 5)
        NEG, NOT_CAUSAL, TAKEN = -3.0e38, -3.4e38, -3.2e38

        def even_slots(g, o):
            return (g // 2, 4 + g // 2 % 2, g // 2) if g % 2 else None

        def cross_slots(g, o):
            return 2 * g + o, 4 + o, 2 * g + o

        @block.sync
        def _(sp):
            sp.dma_start(h[:, 1, :], x[P:2 * P, :]).then_inc(x_in[1], 16)
            sp.dma_start(h[:, 3, :], x[3 * P:4 * P, :]).then_inc(x_in[3], 16)
            sp.dma_start(w_raw[:, 0, :], wstream[0]).then_inc(w_in[0], 16)
            sp.dma_start(w_raw[:, 1, :], wstream[1]).then_inc(w_in[1], 16)
            with sp.Fori(1, NU // 2) as i:
                for s in range(2):
                    sp.wait_ge(w_ready, 2 * i + (s - 1))
                    sp.dma_start(w_raw[:, s:s + 1, :], wstream[bass.ds(2 * i + s, 1)].rearrange("o p c -> p o c"))\
                        .then_inc(w_in[s], 16)
            if NU % 2:
                sp.wait_ge(w_ready, NU - 2)
                sp.dma_start(w_raw[:, (NU - 1) % 2, :], wstream[NU - 1]).then_inc(w_in[(NU - 1) % 2], 16)
            for t in range(TT):
                sp.wait_ge(h_ready, TT * (NP - 1) + t + 1)
                sp.dma_start(out[t * P:(t + 1) * P, :], h[:, t, :]).then_inc(out_done, 16)
            sp.wait_ge(out_done, 16 * TT)

        @block.gpsimd
        def _(pool):
            nc.gpsimd.memset(ident[:, :], 0.0).then_inc(consts, 1)
            nc.gpsimd.memset(ones[:, :], 1.0).then_inc(consts, 1)
            nc.gpsimd.memset(eps[:, 0:1], EPS).then_inc(consts, 1)
            nc.gpsimd.memset(eps[:, 1:2], 4 * EPS).then_inc(consts, 1)
            pool.wait_ge(consts, 4)
            nc.gpsimd.affine_select(out=ident[:, :], in_=ident[:, :], compare_op=ALU.not_equal, fill=1.0,
                                    base=0, pattern=[[-1, P]], channel_multiplier=1).then_inc(consts, 1)

            def even(i):
                count = [0]

                def link(ins):
                    count[0] += 1
                    ins.then_inc(e["pool_link"], 1)
                    pool.wait_ge(e["pool_link"], count[0])

                nc.gpsimd.memset(e_bd[:, :, :, :], 0.0).then_inc(e["bd0"], 1)
                nc.gpsimd.memset(e_xb[:, :, 0:CONV - 1], 0.0).then_inc(e["pad"], 1)
                link(nc.gpsimd.memset(e_tri[:, :], 0.0))
                nc.gpsimd.affine_select(out=e_tri[:, :], in_=e_tri[:, :], compare_op=ALU.is_ge, fill=NEG, base=0,
                                        pattern=[[-1, P]], channel_multiplier=1).then_inc(e["tri"], 1)
                for b in range(1, TT):
                    pool.wait_ge(e["acc"], IH * b)
                    diag = e_sc[:, b - 1, b * P:(b + 1) * P]
                    nc.gpsimd.affine_select(out=diag, in_=diag, compare_op=ALU.is_ge, fill=NOT_CAUSAL, base=0,
                                            pattern=[[-1, P]], channel_multiplier=1).then_inc(e["filled"], 1)
                for c in range(LRUT):
                    pool.wait_ge(p_free, PT0[i, "x_b"] + c + 3)
                    w0 = COLS["conv_w"] + c * CONV
                    b0 = COLS["conv_b"] + c
                    for k in range(CONV):
                        if k == 0:
                            link(nc.gpsimd.tensor_scalar(e_xc[:, c, :], e_xb[:, c, 0:SEQ], col[:, w0:w0 + 1],
                                                         col[:, b0:b0 + 1], ALU.mult, ALU.add))
                        else:
                            link(nc.gpsimd.tensor_tensor(tmp[:, 3, :], e_xb[:, c, k:k + SEQ],
                                                         col[:, w0 + k:w0 + k + 1].to_broadcast([P, SEQ]), ALU.mult))
                            ins = nc.gpsimd.tensor_tensor(e_xc[:, c, :], e_xc[:, c, :], tmp[:, 3, :], ALU.add)
                            if k < CONV - 1:
                                link(ins)
                            else:
                                ins.then_inc(e["conv"], 1)
                for c in range(LRUT):
                    pool.wait_ge(e["sig"], 2 * LRUT)
                    nc.gpsimd.tensor_tensor(e_xc[:, c, :], e_xc[:, c, :], f_i[:, c, :], ALU.mult)\
                        .then_inc(e["t2"], 1)

            def gla(i):
                nc.gpsimd.memset(g_keep[:, :], 1.0).then_inc(gs["keep"], 1)
                pool.wait_ge(gs["keep"], 1)
                nc.gpsimd.memset(g_keep[:, :].rearrange("p (c t) -> p c t", t=CH)[:, :, 0:1], 0.0)\
                    .then_inc(gs["keep"], 1)
                nc.gpsimd.memset(g_mask[:, :], 1.0).then_inc(gs["mask"], 1)
                pool.wait_ge(gs["mask"], 1)
                nc.gpsimd.affine_select(out=g_mask[:, :], in_=g_mask[:, :], compare_op=ALU.is_ge, fill=0.0, base=0,
                                        pattern=[[1, P]], channel_multiplier=-1).then_inc(gs["mask"], 1)
                pool.wait_ge(gs["mask"], 2)
                nc.gpsimd.memset(g_mask[0:CH, CH:P], 0.0).then_inc(gs["mask"], 1)
                nc.gpsimd.memset(g_att[:, :, :], 0.0).then_inc(gs["zero"], 1)

            for i in range(NP):
                if i > 0 and parts[i][0] in ("even", "gla"):
                    pool.wait_ge(h_ready, TT * i)
                if parts[i][0] == "even":
                    even(i)
                elif parts[i][0] == "gla":
                    gla(i)

        @block.scalar
        def _(act):
            nc.scalar.dma_start(h[:, 0, :], x[0:P, :]).then_inc(x_in[0], 16)
            nc.scalar.dma_start(gain_bc[:, :], gains[0:1, :].to_broadcast([P, DM])).then_inc(gain_in, 16)
            nc.scalar.dma_start(h[:, 2, :], x[2 * P:3 * P, :]).then_inc(x_in[2], 16)
            nc.scalar.dma_start(col[:, :], cols).then_inc(cols_in, 16)
            act.sem_inc(p_free, 2)

            def post_root(i, pair):
                half = parts[i - 1][0] == "ffn"
                act.wait_ge(ssq_ready, 2 * (i - 1) + pair + 1)
                nc.scalar.activation(stat[:, i, 4 + 2 * pair:6 + 2 * pair], stat[:, i, 2 * pair:2 * pair + 2], ACT.Sqrt,
                                     scale=(4.0 if half else 1.0) / DM,
                                     bias=eps[:, 1:2] if half else eps[:, 0:1]).then_inc(root_ready, 1)

            def norm(i):
                if i == 0:
                    act.preload_act_table(ACT.Sqrt)
                    act.wait_ge(consts, 5)

                def root(pair):
                    act.wait_ge(h_sq, TT * i + 2 * pair + 2)
                    at = slice(16 + 2 * pair, 18 + 2 * pair)
                    nc.scalar.activation(stat[:, i, at], stat[:, i, 12 + 2 * pair:14 + 2 * pair], ACT.Sqrt,
                                         scale=1.0 / DM, bias=eps[:, 0:1]).then_inc(root_ready, 1)

                def square(t):
                    if i > 0:
                        act.wait_ge(o_sq, 2 * TT * i)
                        act.wait_ge(h_ready, TT * (i - 1) + t + 1)
                    else:
                        act.wait_ge(x_in[t], 16)
                    if i + t > 0:
                        act.wait_ge(h_sq, TT * i + t)
                    nc.scalar.activation(tmp[:, 0:2, :].rearrange("p a b -> p (a b)"), h[:, t, :], ACT.Square,
                                         accum_out=stat[:, i, 12 + t:13 + t]).then_inc(h_sq, 1)

                def upper(t):
                    for b in range(2):
                        act.wait_ge(xT_ready, 2 * TT * i + 2 * t + b + 1)
                        nc.scalar.activation(x_hi[:, 4 * b:4 * b + 4, t * P:(t + 1) * P],
                                             bank(4 + 2 * (t % 2) + b).rearrange("p (k c) -> p k c", k=4),
                                             ACT.Copy).then_inc(x_hi_ready, 1)
                def key(k):
                    u = U[i, "k"] + k
                    act.wait_ge(w_free, u + 3)
                    nc.scalar.activation(c_kT[:, k, :], bank((PT0[i, "k"] + k) % 2)[:, 0:NMEM], ACT.Copy)\
                        .then_inc(p_free, 1)
                    split_hi(act, u + 2, u % 2)

                if parts[i][0] == "cross":
                    square(0)
                    square(1)
                    root(0)
                    post_root(i, 1)
                    key(0)
                    key(1)
                    square(2)
                    key(2)
                    key(3)
                    square(3)
                    root(1)
                    key(4)
                    upper(0)
                    key(5)
                    key(6)
                    upper(1)
                    key(7)
                    upper(2)
                    split_units(i, "v", 2)
                else:
                    square(0)
                    square(1)
                    root(0)
                    if i > 0:
                        post_root(i, 1)
                    upper(0)
                    square(2)
                    upper(1)
                    square(3)
                    root(1)
                    if i == 0:
                        split_hi(act, 0, 0)
                    upper(2)
                    if i == 0:
                        split_hi(act, 1, 1)
                    upper(3)
                if i == 0:
                    act.wait_ge(cols_in, 16)
                if i + 1 < NP:
                    act.wait_ge(xs_ready, TT * (i + 1))
                    nc.scalar.dma_start(gain_bc[:, :], gains[i + 1:i + 2, :].to_broadcast([P, DM]))\
                        .then_inc(gain_in, 16)
                return upper

            def ffn(i):
                n0, u0 = nffn[i] * FT, U[i, "gate_up"]
                act.preload_act_table(ACT.Silu)
                with act.Fori(0, FT // 2) as it:
                    for jj in range(2):
                        j = 2 * it + jj
                        split_hi(act, 2 * j + (u0 + 2), u0 % 2)
                        act.wait_ge(w_free, 2 * j + (u0 + 4))
                        act.wait_ge(act_ready, j + (n0 + 1))
                        nc.scalar.activation(tmp[:, jj, :], bank(2 * jj), ACT.Silu).then_inc(silu_ready, 1)
                        split_hi(act, 2 * j + (u0 + 3), (u0 + 1) % 2)
                        act.wait_ge(gu_free, j + (n0 + 3))
                        nc.scalar.activation(act_hi[:, bass.ds(j, 1), :], tmp[:, jj:jj + 1, :], ACT.Copy)\
                            .then_inc(act_hi_ready, 1)
                output(i, "down", FT // 2)

            def mem_load(i):
                layer = parts[i + 1][1]
                if parts[i][0] == "even":
                    act.wait_ge(at_olo, O0[i] + AH // 2)
                else:
                    act.wait_ge(gs["y_ready"], 2 * TT)
                nc.scalar.dma_start(c_mem[:, :, :], mem.rearrange("(m p) d -> p m d", p=P)).then_inc(mem_in, 16)
                nc.scalar.dma_start(c_gain[:, :], mem_gains[layer:layer + 1, :].to_broadcast([P, DM]))\
                    .then_inc(mem_in, 16)

            def mem_norm(i):
                c = ncross[i + 1]
                act.wait_ge(mem_in, 32 * (c + 1))
                for m in range(MT):
                    nc.scalar.activation(c_v[:, m, :], c_mem[:, m, :], ACT.Square, accum_out=c_stat[:, m:m + 1])\
                        .then_inc(mem_sq, 1)
                act.wait_ge(mem_sq, MT * (c + 1))
                nc.scalar.activation(c_stat[:, 4:4 + MT], c_stat[:, 0:MT], ACT.Sqrt, scale=1.0 / DM,
                                     bias=eps[:, 0:1]).then_inc(mem_root, 1)

            def mem_upper(i):
                c = ncross[i + 1]
                for m in range(MT):
                    for b in range(2):
                        act.wait_ge(memT_ready, 4 * c + 2 * m + b + 1)
                        nc.scalar.activation(c_mem_hi[:, 4 * b:4 * b + 4, m * P:(m + 1) * P],
                                             bank(4 + 2 * m + b).rearrange("p (k c) -> p k c", k=4), ACT.Copy)\
                            .then_inc(memT_hi, 1)

            def output(i, seg, nu):
                u0 = U[i, seg]
                mem_next = i + 1 < NP and parts[i + 1][0] == "cross"
                if mem_next:
                    mem_load(i)
                act.preload_act_table(ACT.Sqrt)
                if parts[i][0] == "ffn":
                    act.wait_ge(act_ready, (nffn[i] + 1) * FT + 2)
                nc.scalar.dma_start(tmp[:, 2:4, :].rearrange("p a b -> p (a b)"),
                                    post_gains[i:i + 1, :].to_broadcast([P, DM])).then_inc(post_in, 16)

                def square(hf, t):
                    if t < TT - 1:
                        act.wait_ge(o_full, (TT - 1) * (2 * i + hf) + t + 1)
                    else:
                        act.wait_ge(w_free, u0 + nu * (hf + 1) + 2)
                    if TT * 2 * i + TT * hf + t > 0:
                        act.wait_ge(o_sq, TT * (2 * i + hf) + t)
                    at = 24 + 2 * t + hf
                    nc.scalar.activation(tmp[:, 0, :], bank(4 * (1 - hf) + t), ACT.Square,
                                         accum_out=stat[:, i + 1, at:at + 1]).then_inc(o_sq, 1)

                for hf in range(2):
                    for q in range(nu):
                        v = u0 + nu * hf + q + 2
                        if q == nu - 1:
                            for t in range(TT):
                                square(hf, t)
                                if hf == 1 and t == 2:
                                    post_root(i + 1, 0)
                        if v < NU:
                            split_hi(act, v, v % 2)
                        if mem_next and q == 1:
                            mem_upper(i) if hf else mem_norm(i)
                if i + 1 == NP:
                    post_root(NP, 1)

            def project(i, seg, n, dst, w=SEQ, func=ACT.Copy, at=0, first=0):
                u0, t0 = U[i, seg], PT0[i, seg]
                with act.Fori(first // 2, n // 2) as it:
                    for jj in range(2):
                        j = 2 * it + jj
                        act.wait_ge(w_free, j + (u0 + 3))
                        nc.scalar.activation(dst[:, bass.ds(j, 1), at:at + w],
                                             ps[:, (t0 + jj) % 2:(t0 + jj) % 2 + 1, 0:w], func).then_inc(p_free, 1)
                        split_hi(act, j + (u0 + 2), (u0 + jj) % 2)

            def split_units(i, seg, n, off=0):
                for q in range(n):
                    v = U[i, seg] + off + q + 2
                    split_hi(act, v, v % 2)

            def attend(i, heads, p, st, scale, slots, out_banks, nk, direct, beside=None):
                a0, o0 = A0[i], O0[i]
                N = heads * TT
                for step in range(N + 1):
                    if step < N:
                        act.wait_ge(at_sm, a0 + step + 1)
                        c = (step % 4) * 4
                        w = nk(step % TT) * P
                        dst = p[:, step % 3, 0:w]
                        nc.scalar.activation(dst, bank(step % 2)[:, 0:w] if direct else dst,
                                             ACT.Exp, bias=st[:, c + 1:c + 2], scale=scale,
                                             accum_out=st[:, c + 2:c + 3]).then_inc(at_e, 1)
                    if beside is not None:
                        beside(step)
                    if step > 0 and (step - 1) % TT == 1 and (step - 1) // TT >= 1:
                        g = (step - 1) // TT - 1
                        for o in range(out_banks):
                            if slots(g, o) is not None:
                                upper_out(i, g, o, slots)
                g = heads - 1
                for o in range(out_banks):
                    if slots(g, o) is not None:
                        upper_out(i, g, o, slots)

            def upper_out(i, g, o, slots):
                k, b, idx = slots(g, o)
                act.wait_ge(at_o, O0[i] + idx + 1)
                nc.scalar.activation(x_hi[:, k, :], bank(b), ACT.Copy).then_inc(at_ohi, 1)

            def cross(i, upper):
                for hf in range(2):
                    if hf == 0:
                        split_units(i, "v", 2, 2)
                    else:
                        upper(TT - 1)
                        split_units(i, "v", 4, 4)
                    act.wait_ge(w_free, U[i, "v"] + 4 * hf + 6)
                    nc.scalar.activation(c_v[:, :, hf * SEQ:(hf + 1) * SEQ], ps[:, 2 - 2 * hf:4 - 2 * hf, :], ACT.Copy)\
                        .then_inc(v_ready, 1)
                act.preload_act_table(ACT.Exp)
                project(i, "q", KT, c_qT)
                attend(i, XH, c_p, c_stat[:, 8:32], XD ** -0.5, cross_slots, 2, lambda t: MT, True)
                output(i, "out", KT // 2)

            def even(i):
                u0 = U[i, "q_idx"]
                act.wait_ge(e["bd0"], 1)
                for n, w in enumerate((w_ra, w_ri)):
                    for q in range(2):
                        nc.scalar.dma_start(e_bd[q * CH:(q + 1) * CH, n, :, q * CH:(q + 1) * CH],
                                            w.rearrange("(c q) i j -> q i c j", q=2)[q]).then_inc(e["bd"], 16)
                act.preload_act_table(ACT.Exp)
                lam = col[:, COLS["lam"]:COLS["lam"] + LRUT]
                nc.scalar.activation(e_lam[:, 0, :], lam, ACT.Abs).then_inc(e["lam_abs"], 1)
                act.wait_ge(e["lam_abs"], 1)
                nc.scalar.activation(e_lam[:, 1, :], e_lam[:, 0, :], ACT.Exp, scale=-1.0).then_inc(e["lam_exp"], 1)
                project(i, "q_idx", 4, e_qi)
                project(i, "c_kv", 2, e_ck)
                act.wait_ge(p_free, PT0[i, "c_kv"] + 4)
                for k in range(2):
                    nc.scalar.activation(tmp[:, k, :], e_ck[:, k, :], ACT.Square).then_inc(e["sq"], 1)
                act.wait_ge(w_free, U[i, "kw_idx"] + 3)
                b = PT0[i, "kw_idx"] % 2
                nc.scalar.activation(e_k2[0:ID, :], bank(b)[0:ID, :], ACT.Copy)
                nc.scalar.activation(e_k2[ID:2 * ID, :], bank(b)[0:ID, :], ACT.Copy)
                nc.scalar.activation(e_wi[:, :], bank(b)[ID:ID + IH, :], ACT.Copy).then_inc(p_free, 1)
                split_units(i, "kw_idx", 1)

                def latent(n):
                    if n == 2:
                        act.wait_ge(e["ms"], 1)
                        nc.scalar.activation(e_t[:, 1, :], tmp[:, 2, :], ACT.Sqrt).then_inc(e["rs"], 1)
                    elif n in (12, 15):
                        k = (n - 12) // 3
                        act.wait_ge(e["ckn"], k + 1)
                        nc.scalar.activation(e_ck_hi[:, k, :], e_ck[:, k, :], ACT.Copy).then_inc(e["ck_hi"], 1)

                for n in range((TT - 1) * IH):
                    w = (n // IH + 2) * P
                    act.wait_ge(e["s"], n + 1)
                    if n >= 2:
                        act.wait_ge(e["acc"], n - 1)
                    nc.scalar.activation(tmp[:, n % 2, 0:w], bank(2 + n % 2)[:, 0:w], ACT.Relu).then_inc(e["relu"], 1)
                    latent(n)
                act.wait_ge(e["pad"], 1)
                project(i, "x_b", 4, e_xb, at=CONV - 1)
                for n in range(4):
                    if n < 3:
                        act.wait_ge(e["uk_full"], n + 1)
                    else:
                        act.wait_ge(w_free, U[i, "uk"] + 3)
                    nc.scalar.activation(e_kT[:, n, :], bank((PT0[i, "uk"] + n) % 2), ACT.Copy).then_inc(p_free, 1)
                split_units(i, "uk", 2)
                act.wait_ge(w_free, U[i, "uv"] + 3)
                nc.scalar.activation(e_v[:, :, :], ps[:, 4:8, :], ACT.Copy).then_inc(v_ready, 1)
                project(i, "gate", 4, e_gate)
                act.preload_act_table(ACT.Sigmoid)
                for n, (dst, bias) in enumerate(((f_r, COLS["b_ra"]), (f_i, COLS["b_ri"]))):
                    for c in range(LRUT):
                        act.wait_ge(e["gates"], n * LRUT + c + 1)
                        nc.scalar.activation(dst[:, c, :], bank(gate_bank[n * LRUT + c]), ACT.Sigmoid,
                                             bias=col[:, bias + c:bias + c + 1]).then_inc(e["sig"], 1)
                act.preload_act_table(ACT.Exp)
                act.wait_ge(e["lam"], 1)
                act.wait_ge(e["conv"], LRUT)
                for c in range(LRUT):
                    act.wait_ge(e["sig"], c + 1)
                    nc.scalar.activation(tmp[:, c, :], f_r[:, c, :], ACT.Exp, scale=e_lam[:, 7, c:c + 1])\
                        .then_inc(e["exp"], 1)
                    act.wait_ge(e["exp"], c + 1)
                    nc.scalar.activation(f_r[:, c, :], f_r[:, c, :], ACT.Tanh, scale=e_lam[:, 6, c:c + 1])\
                        .then_inc(e["tanh"], 1)
                project(i, "q", 2, e_qT)
                for c in range(LRUT):
                    nc.scalar.activation(e_gate[:, c, :], e_gate[:, c, :], ACT.Gelu_apprx_tanh).then_inc(e["gelu"], 1)
                project(i, "q", 4, e_qT, first=2)
                act.preload_act_table(ACT.Exp)

                def recurrence_steps(step):
                    if step == 11:
                        act.wait_ge(e["bv"], LRUT)
                        act.wait_ge(e["tanh"], LRUT)
                        for c in range(LRUT):
                            nc.scalar.activation(f_r[:, c, :], f_r[:, c, :], ACT.Sqrt, scale=4.0)\
                                .then_inc(e["sqrt"], 1)
                        act.preload_act_table(ACT.Exp)
                    c, k = divmod(step - 13, 5)
                    if k == 3 and 0 <= c < LRUT:
                        act.wait_ge(e["y"], c + 1)
                        nc.scalar.activation(x_hi[:, 4 + c, :], e_xc[:, c, :], ACT.Copy).then_inc(e["y_hi"], 1)

                attend(i, AH, e_p, e_st, AD ** -0.5, even_slots, 1, lambda t: t + 1, False, recurrence_steps)
                output(i, "out", KT // 2)

            def gla(i):
                nc.scalar.dma_start(g_w2[:, :], w_g2).then_inc(gs["w2_in"], 16)
                nc.scalar.dma_start(g_gain[:, :], head_gain.to_broadcast([P, GDV])).then_inc(gs["gain_in"], 16)
                act.preload_act_table_set("natural_log_exp_and_others")
                act.wait_ge(w_free, U[i, "g_lr"] + 3)
                nc.scalar.activation(g_lr[:, :], bank(PT0[i, "g_lr"] % 2)[0:GR, :], ACT.Copy).then_inc(p_free, 1)
                split_units(i, "g_lr", 1)
                project(i, "q", GH, g_q)
                for n in range(GH):
                    c = COLS["b_g"] + n
                    act.wait_ge(gs["z_full"], n + 1)
                    nc.scalar.activation(g_kr[:, n, :], bank(4 + n), ACT.Identity, bias=col[:, c:c + 1])\
                        .then_inc(gs["z"], 1)
                project(i, "k", GH, g_k)
                act.wait_ge(p_free, PT0[i, "k"] + GH + 2)
                act.preload_act_table_set("natural_log_exp_and_others")
                for n in range(GH):
                    split_units(i, "v", 1, 2 * n)
                    act.wait_ge(gs["z"], n + 1)
                    if n > 0:
                        act.wait_ge(gs["G"], 2 * n)
                    nc.scalar.activation(tmp[:, 0, :], g_kr[:, n, :], ACT.Abs).then_inc(gs["abs"], 1)
                    act.wait_ge(gs["abs"], n + 1)
                    nc.scalar.activation(tmp[:, 0, :], tmp[:, 0, :], ACT.Exp, scale=-1.0).then_inc(gs["exp"], 1)
                    act.wait_ge(gs["exp"], n + 1)
                    nc.scalar.activation(tmp[:, 0, :], tmp[:, 0, :], ACT.Ln, bias=1.0).then_inc(gs["ln"], 1)
                    if n == 2:
                        act.wait_ge(w_free, U[i, "v"] + 6)
                        nc.scalar.activation(g_v[:, :, 0:SEQ], ps[:, 4:8, :], ACT.Copy).then_inc(v_ready, 1)
                    act.wait_ge(gs["G"], 2 * n + 2)
                    if n > 0:
                        act.wait_ge(gs["qk"], 3 * n)
                    nc.scalar.activation(g_t[:, 0, :], tmp[:, 2, :], ACT.Exp, scale=1.0 / 16)
                    nc.scalar.activation(g_t[:, 1, :], tmp[:, 2, :], ACT.Exp, scale=-1.0 / 16).then_inc(gs["e"], 1)
                    nc.scalar.activation(tmp[:, 3, :], tmp[:, 3, :], ACT.Exp, scale=1.0 / 16).then_inc(gs["e"], 1)
                    split_units(i, "v", 1, 2 * n + 1)
                act.wait_ge(w_free, U[i, "v"] + 10)
                nc.scalar.activation(g_v[:, :, SEQ:2 * SEQ], ps[:, 0:4, :], ACT.Copy).then_inc(v_ready, 1)
                for n in range(GH):
                    act.wait_ge(gs["krT"], n + 1)
                    nc.scalar.activation(g_krt[:, :, n, :], bank(4 + n).rearrange("p (t c) -> p t c", t=TT), ACT.Copy)\
                        .then_inc(gs["krt"], 1)
                act.preload_act_table(ACT.Silu)
                project(i, "r", KT, g_r, func=ACT.Silu)
                act.preload_act_table(ACT.Sqrt)
                for w in range(TT * GH):
                    T, n = w // GH, w % GH
                    act.wait_ge(gs["o_full"], w + 1)
                    nc.scalar.activation(f[:, T, n * GDV:(n + 1) * GDV], bank(4 + w % 2)[:, 0:GDV], ACT.Copy)
                    if w > 0:
                        act.wait_ge(gs["osq"], w)
                    nc.scalar.activation(tmp[:, 2, 0:GDV], bank(4 + w % 2)[:, 0:GDV], ACT.Square,
                                         accum_out=g_st[:, 0, w:w + 1]).then_inc(gs["osq"], 1)
                    if n == GH - 1:
                        act.wait_ge(gs["osq"], w + 1)
                        nc.scalar.activation(g_st[:, 3, GH * T:GH * (T + 1)], g_st[:, 0, GH * T:GH * (T + 1)],
                                             ACT.Sqrt, scale=1.0 / GDV, bias=eps[:, 0:1]).then_inc(gs["root"], 1)
                for T in range(TT):
                    for b in range(2):
                        act.wait_ge(gs["y"], 2 * T + b + 1)
                        nc.scalar.activation(x_hi[:, 4 * b:4 * b + 4, T * P:(T + 1) * P],
                                             tmp[:, 2 * (T % 2) + b, :].rearrange("p (k c) -> p k c", k=4), ACT.Copy)\
                            .then_inc(gs["y_hi"], 1)
                output(i, "out", KT // 2)

            for i in range(NP):
                upper = norm(i)
                if parts[i][0] == "ffn":
                    ffn(i)
                elif parts[i][0] == "cross":
                    cross(i, upper)
                elif parts[i][0] == "even":
                    even(i)
                else:
                    gla(i)

        @block.vector
        def _(dve):
            dve.sem_inc(gu_free, 2)
            dve.sem_inc(act_ready, 2)
            link_count = [0]

            def link(ins):
                link_count[0] += 1
                ins.then_inc(stat_link, 1)
                dve.wait_ge(stat_link, link_count[0])

            def norm(i):
                def store(t):
                    store_half(i - 1, 1, t)

                def sums(pair):
                    at, to = 24 + 4 * pair, 2 * pair
                    sq = stat[:, i, at:at + 4].rearrange("p (t h) -> p t h", h=2)
                    nc.vector.tensor_tensor(stat[:, i, to:to + 2], sq[:, :, 0], sq[:, :, 1], ALU.add)\
                        .then_inc(ssq_ready, 1)
                    dve.wait_ge(ssq_ready, 2 * (i - 1) + pair + 1)
                    half = 4.0 if parts[i - 1][0] == "ffn" else 1.0
                    inv = stat[:, i, 8 + to:10 + to]
                    link(nc.vector.tensor_scalar(inv, stat[:, i, to:to + 2], half / DM, half * EPS, ALU.mult, ALU.add))
                    link(nc.vector.reciprocal(inv, inv))

                def rstd(pair):
                    to = 2 * pair
                    dve.wait_ge(root_ready, 4 * i - 1 if pair == 0 else 4 * i if i == NP else 4 * i + 1)
                    inv = stat[:, i, 8 + to:10 + to]
                    link(nc.vector.tensor_tensor(inv, inv, stat[:, i, 4 + to:6 + to], ALU.mult))

                def update(t):
                    if i > 0:
                        nc.vector.scalar_tensor_tensor(h[:, t, :], f[:, t, :], stat[:, i, 8 + t:9 + t], h[:, t, :],
                                                       ALU.mult, ALU.add).then_inc(h_ready, 1)

                def mean(pair):
                    dve.wait_ge(h_sq, TT * i + 2 * pair + 2)
                    inv = stat[:, i, 20 + 2 * pair:22 + 2 * pair]
                    link(nc.vector.tensor_scalar(inv, stat[:, i, 12 + 2 * pair:14 + 2 * pair], 1.0 / DM, EPS,
                                                 ALU.mult, ALU.add))
                    link(nc.vector.reciprocal(inv, inv))
                    dve.wait_ge(root_ready, 4 * i + 2 if pair else max(4 * i, 1))
                    link(nc.vector.tensor_tensor(inv, inv, stat[:, i, 16 + 2 * pair:18 + 2 * pair], ALU.mult))

                def scale(t):
                    if t == 0:
                        dve.wait_ge(gain_in, 16 * (i + 1))
                    if i == 0:
                        dve.wait_ge(x_in[t], 16)
                    nc.vector.scalar_tensor_tensor(f[:, t, :], h[:, t, :], stat[:, i, 20 + t:21 + t], gain_bc[:, :],
                                                   ALU.mult, ALU.mult).then_inc(xs_ready, 1)

                def lower(t):
                    for b in range(2):
                        dve.wait_ge(x_hi_ready, 2 * TT * i + 2 * t + b + 1)
                        xh = x_hi[:, 4 * b:4 * b + 4, t * P:(t + 1) * P]
                        nc.vector.tensor_tensor(x_lo[:, 4 * b:4 * b + 4, t * P:(t + 1) * P],
                                                bank(4 + 2 * (t % 2) + b).rearrange("p (k c) -> p k c", k=4),
                                                xh.bitcast(f32), ALU.subtract).then_inc(x_ready, 1)

                if i > 0:
                    store(0)
                    store(1)
                    sums(0)
                    store(2)
                    rstd(0)
                def split_second():
                    v = U[i, UNITS[parts[i][0]][0][0]] + 1
                    split_lo(dve, v, v % 2)

                update(0)
                if i < NP and parts[i][0] == "cross":
                    split_second()
                update(1)
                if i > 0:
                    store(3)
                    sums(1)
                if i == NP:
                    rstd(1)
                    update(2)
                    update(3)
                    return
                if parts[i][0] == "cross":
                    def keys(k, n=1):
                        for q in range(k, k + n):
                            split_lo(dve, U[i, "k"] + q + 2, (U[i, "k"] + q) % 2)

                    keys(0)
                    rstd(1)
                    update(2)
                    keys(1)
                    mean(0)
                    scale(0)
                    keys(2)
                    scale(1)
                    keys(3)
                    update(3)
                    keys(4)
                    lower(0)
                    keys(5)
                    mean(1)
                    scale(2)
                    keys(6)
                    lower(1)
                    keys(7)
                    lower(2)
                    keys(8)
                    scale(3)
                    keys(9)
                    return lower
                mean(0)
                scale(0)
                scale(1)
                if i > 0:
                    rstd(1)
                update(2)
                lower(0)
                update(3)
                lower(1)
                if i > 0:
                    split_second()
                mean(1)
                scale(2)
                scale(3)
                if i == 0:
                    split_lo(dve, 0, 0)
                lower(2)
                if i == 0:
                    split_lo(dve, 1, 1)
                lower(3)

            def ffn(i):
                n0, u0 = nffn[i] * FT, U[i, "gate_up"]
                with dve.Fori(0, FT // 2) as it:
                    for jj in range(2):
                        j = 2 * it + jj
                        split_lo(dve, 2 * j + (u0 + 2), u0 % 2)
                        dve.wait_ge(silu_ready, j + (n0 + 1))
                        nc.vector.tensor_tensor(tmp[:, jj, :], bank(2 * jj + 1), tmp[:, jj, :], ALU.mult)\
                            .then_inc(gu_free, 1)
                        split_lo(dve, 2 * j + (u0 + 3), (u0 + 1) % 2)
                        dve.wait_ge(act_hi_ready, j + (n0 + 1))
                        nc.vector.tensor_tensor(act_lo[:, bass.ds(j, 1), :], tmp[:, jj:jj + 1, :],
                                                act_hi[:, bass.ds(j, 1), :].bitcast(f32), ALU.subtract)\
                            .then_inc(act_ready, 1)
                output(i, "down", FT // 2)

            def mem_norm(i):
                c = ncross[i + 1]
                dve.wait_ge(mem_sq, MT * (c + 1))
                inv = c_stat[:, 2:2 + MT]
                link(nc.vector.tensor_scalar(inv, c_stat[:, 0:MT], 1.0 / DM, EPS, ALU.mult, ALU.add))
                link(nc.vector.reciprocal(inv, inv))
                dve.wait_ge(mem_root, c + 1)
                link(nc.vector.tensor_tensor(inv, inv, c_stat[:, 4:4 + MT], ALU.mult))
                for m in range(MT):
                    nc.vector.scalar_tensor_tensor(c_mem[:, m, :], c_mem[:, m, :], c_stat[:, 2 + m:3 + m],
                                                   c_gain[:, :], ALU.mult, ALU.mult).then_inc(mem_n, 1)

            def mem_lower(i):
                c = ncross[i + 1]
                for m in range(MT):
                    for b in range(2):
                        dve.wait_ge(memT_hi, 4 * c + 2 * m + b + 1)
                        nc.vector.tensor_tensor(c_mem_lo[:, 4 * b:4 * b + 4, m * P:(m + 1) * P],
                                                bank(4 + 2 * m + b).rearrange("p (k c) -> p k c", k=4),
                                                c_mem_hi[:, 4 * b:4 * b + 4, m * P:(m + 1) * P].bitcast(f32),
                                                ALU.subtract).then_inc(memT_used, 1)

            def store_half(i, hf, t):
                dve.wait_ge(o_sq, TT * (2 * i + hf) + t + 1)
                dve.wait_ge(post_in, 16 * (i + 1))
                nc.vector.tensor_tensor(f[:, t, hf * SEQ:(hf + 1) * SEQ], bank(4 * (1 - hf) + t), tmp[:, 2 + hf, :],
                                        ALU.mult).then_inc(f_ready, 1)

            def output(i, seg, nu):
                u0 = U[i, seg]
                mem_next = i + 1 < NP and parts[i + 1][0] == "cross"
                for hf in range(2):
                    for q in range(nu if hf == 0 else nu - 1):
                        v = u0 + nu * hf + q + 2
                        if q == nu - 1:
                            for t in range(TT):
                                store_half(i, 0, t)
                        if v < NU:
                            split_lo(dve, v, v % 2)
                        if mem_next and q == 1:
                            mem_lower(i) if hf else mem_norm(i)

            def project(i, seg, n):
                u0 = U[i, seg]
                with dve.Fori(0, n // 2) as it:
                    for jj in range(2):
                        split_lo(dve, 2 * it + (u0 + 2 + jj), (u0 + jj) % 2)

            def split_units(i, seg, n, off=0):
                for q in range(n):
                    v = U[i, seg] + off + q + 2
                    split_lo(dve, v, v % 2)

            def attend(i, heads, p, pT, st, scale, slots, out_banks, nk, bias, beside=None):
                a0 = A0[i]
                N = heads * TT

                def lower_out(g):
                    for o in range(out_banks):
                        if slots(g, o) is not None:
                            k, b, idx = slots(g, o)
                            dve.wait_ge(at_ohi, O0[i] + idx + 1)
                            nc.vector.tensor_tensor(x_lo[:, k, :], bank(b), x_hi[:, k, :].bitcast(f32), ALU.subtract)\
                                .then_inc(at_olo, 1)

                for step in range(N + 2):
                    if step < N:
                        w = nk(step % TT) * P
                        c = (step % 4) * 4
                        dve.wait_ge(at_s, a0 + step + 1)
                        if step >= 3:
                            dve.wait_ge(at_t, a0 + step - 2)
                        if bias is None:
                            link(nc.vector.tensor_reduce(st[:, c:c + 1], bank(step % 2)[:, 0:w], AX.X, ALU.max))
                        else:
                            link(nc.vector.tensor_tensor_reduce(
                                out=p[:, step % 3, 0:w], in0=bank(step % 2)[:, 0:w], in1=bias(step % TT),
                                scale=1.0, scalar=-3.0e38, op0=ALU.add, op1=ALU.max, accum_out=st[:, c:c + 1]))
                        nc.vector.tensor_scalar(st[:, c + 1:c + 2], st[:, c:c + 1], -scale, None, ALU.mult)\
                            .then_inc(at_sm, 1)
                    if 1 <= step < N + 1:
                        s1 = step - 1
                        w = nk(s1 % TT) * P
                        c = (s1 % 4) * 4
                        dve.wait_ge(at_e, a0 + s1 + 1)
                        link(nc.vector.reciprocal(st[:, c + 3:c + 4], st[:, c + 2:c + 3]))
                        nc.vector.tensor_scalar(p[:, s1 % 3, 0:w], p[:, s1 % 3, 0:w], st[:, c + 3:c + 4], None,
                                                ALU.mult).then_inc(at_p, 1)
                    if step >= 2:
                        s2 = step - 2
                        g, t = s2 // TT, s2 % TT
                        dve.wait_ge(at_t, a0 + s2 + 1)
                        k = nk(t)
                        nc.vector.tensor_copy(pT[:, g % 2, 0:k, t * P:(t + 1) * P],
                                              bank(2 + s2 % 2)[:, 0:k * P].rearrange("p (k c) -> p k c", k=k))\
                            .then_inc(at_pT, 1)
                        if t == 2 and g >= 1:
                            lower_out(g - 1)
                        if beside is not None:
                            beside(step)
                lower_out(heads - 1)

            def cross(i, lower):
                split_units(i, "v", 2, 2)
                lower(TT - 1)
                split_units(i, "v", KT - 4, 4)
                project(i, "q", KT)
                attend(i, XH, c_p, c_pT, c_stat[:, 8:32], XD ** -0.5, cross_slots, 2, lambda t: MT, None)
                output(i, "out", KT // 2)

            def even(i):
                L = lambda k: e_lam[:, k, :]
                lam = col[:, COLS["lam"]:COLS["lam"] + LRUT]
                dve.wait_ge(e["lam_exp"], 1)
                link(nc.vector.tensor_scalar(L(2), L(1), 2.0, None, ALU.add))
                link(nc.vector.reciprocal(L(3), L(2)))
                link(nc.vector.tensor_tensor(L(2), L(1), L(3), ALU.mult))
                link(nc.vector.tensor_tensor(L(3), L(2), L(2), ALU.mult))
                link(nc.vector.tensor_scalar(L(4), L(3), 1.0 / 19, 1.0 / 17, ALU.mult, ALU.add))
                for d in (15, 13, 11, 9, 7, 5, 3, 1):
                    link(nc.vector.tensor_tensor(L(5), L(4), L(3), ALU.mult))
                    link(nc.vector.tensor_scalar(L(4), L(5), 1.0 / d, None, ALU.add))
                link(nc.vector.scalar_tensor_tensor(L(5), L(4), 2.0, L(2), ALU.mult, ALU.mult))
                link(nc.vector.tensor_scalar(L(4), lam, -1.0, 0.0, ALU.mult, ALU.max))
                link(nc.vector.tensor_tensor(L(5), L(4), L(5), ALU.add))
                nc.vector.tensor_scalar(L(6), L(5), 4.0, None, ALU.mult)
                nc.vector.tensor_scalar(L(7), L(5), -8.0, None, ALU.mult).then_inc(e["lam"], 1)

                project(i, "q_idx", 4)
                project(i, "c_kv", 2)
                split_units(i, "kw_idx", 1)

                def latent(n):
                    if n == 1:
                        nc.vector.tensor_scalar(tmp[:, 2, :], bank(4), 1.0 / RANK, EPS, ALU.mult, ALU.add)\
                            .then_inc(e["ms"], 1)
                    elif n == 4:
                        dve.wait_ge(e["ms"], 1)
                        link(nc.vector.reciprocal(e_t[:, 0, :], tmp[:, 2, :]))
                    elif n == 7:
                        dve.wait_ge(e["rs"], 1)
                        link(nc.vector.tensor_tensor(e_t[:, 0, :], e_t[:, 0, :], e_t[:, 1, :], ALU.mult))
                    elif n in (10, 13):
                        k = (n - 10) // 3
                        c = COLS["kv_norm"] + k
                        nc.vector.scalar_tensor_tensor(e_ck[:, k, :], e_ck[:, k, :], col[:, c:c + 1], e_t[:, 0, :],
                                                       ALU.mult, ALU.mult).then_inc(e["ckn"], 1)
                    elif n in (16, 19):
                        k = (n - 16) // 3
                        dve.wait_ge(e["ck_hi"], k + 1)
                        nc.vector.tensor_tensor(e_ck_lo[:, k, :], e_ck[:, k, :], e_ck_hi[:, k, :].bitcast(f32),
                                                ALU.subtract).then_inc(e["ck_ready"], 1)

                dve.wait_ge(e["ssq"], 1)
                dve.wait_ge(e["wT"], 1)
                nc.vector.tensor_scalar(e_w[:, :, :], bank(3)[:, 0:TT * IH].rearrange("p (t c) -> p t c", t=TT),
                                        IH ** -0.5, ID ** -0.5, ALU.mult, ALU.mult).then_inc(e["w"], 1)
                dve.wait_ge(e["w"], 1)
                for n in range((TT - 1) * IH):
                    b, hd = n // IH, n % IH
                    w = (b + 2) * P
                    dve.wait_ge(e["relu"], n + 1)
                    wh = e_w[:, b + 1, hd:hd + 1]
                    if hd == 0:
                        nc.vector.tensor_scalar(e_sc[:, b, 0:w], tmp[:, n % 2, 0:w], wh, None, ALU.mult)\
                            .then_inc(e["acc"], 1)
                    else:
                        dve.wait_ge(e["acc"], n)
                        nc.vector.scalar_tensor_tensor(e_sc[:, b, 0:w], tmp[:, n % 2, 0:w], wh, e_sc[:, b, 0:w],
                                                       ALU.mult, ALU.add).then_inc(e["acc"], 1)
                    latent(n)

                def take(r):
                    per = TOPK // 8
                    if r >= (TT - 1) * per:
                        return
                    b = r // per
                    sc = e_sc[:, b, 0:(b + 2) * P]
                    if r % per == 0:
                        dve.wait_ge(e["filled"], b + 1)
                    link(nc.vector.max(e_max8[:, :], sc))
                    link(nc.vector.match_replace(sc, e_max8[:, :], sc, TAKEN))
                    if r % per == per - 1:
                        link(nc.vector.tensor_scalar(sc, sc, TAKEN, NEG, ALU.not_equal, ALU.mult))

                def factor(c, k):
                    T, R = f_r[:, c, :], tmp[:, c, :]
                    if k == 0:
                        dve.wait_ge(e["tanh"], c + 1)
                        link(nc.vector.tensor_scalar(R, R, 0.5, 0.5, ALU.mult, ALU.add))
                    elif k == 1:
                        link(nc.vector.scalar_tensor_tensor(e_t[:, 0, :], T, 1.0, R, ALU.add, ALU.mult))
                    elif k == 2:
                        link(nc.vector.tensor_scalar(e_t[:, 0, :], e_t[:, 0, :], -1.0, 2.0, ALU.mult, ALU.add))
                    elif k == 3:
                        link(nc.vector.tensor_tensor(R, R, e_t[:, 0, :], ALU.mult))
                    else:
                        dve.wait_ge(e["t2"], c + 1)
                        nc.vector.tensor_scalar(f_i[:, c, :], R, 2.0, -1.0, ALU.mult, ALU.add).then_inc(e["bv"], 1)

                r = 0
                for seg, n in (("x_b", 4), ("uk", 1), ("uv", 1), ("gate", 4), ("q", 4)):
                    for q in range(n):
                        split_units(i, seg, 1, q)
                        for _ in range(4):
                            take(r)
                            r += 1

                def recurrence(step):
                    if step < 12:
                        for n in (2 * step - 4, 2 * step - 3):
                            factor(n // 5, n % 5)
                    c, k = divmod(step - 13, 5)
                    if not 0 <= c < LRUT:
                        return
                    if k == 0:
                        dve.wait_ge(e["sqrt"], c + 1)
                        link(nc.vector.tensor_tensor(e_t[:, 0, :], f_r[:, c, :], tmp[:, c, :], ALU.mult))
                    elif k == 1:
                        dve.wait_ge(e["t2"], c + 1)
                        link(nc.vector.tensor_tensor(e_t[:, 0, :], e_t[:, 0, :], e_xc[:, c, :], ALU.mult))
                    elif k == 2:
                        dve.wait_ge(e["bv"], LRUT)
                        link(nc.vector.tensor_tensor_scan(e_t[:, 1, :], f_i[:, c, :], e_t[:, 0, :], 0.0,
                                                          ALU.mult, ALU.add))
                    elif k == 3:
                        dve.wait_ge(e["gelu"], c + 1)
                        nc.vector.tensor_tensor(e_xc[:, c, :], e_t[:, 1, :], e_gate[:, c, :], ALU.mult)\
                            .then_inc(e["y"], 1)
                    else:
                        dve.wait_ge(e["y_hi"], c + 1)
                        nc.vector.tensor_tensor(x_lo[:, 4 + c, :], e_xc[:, c, :], x_hi[:, 4 + c, :].bitcast(f32),
                                                ALU.subtract).then_inc(e["y_ready"], 1)

                dve.wait_ge(e["tri"], 1)
                attend(i, AH, e_p, e_pT, e_st, AD ** -0.5, even_slots, 1, lambda t: t + 1,
                       lambda t: e_tri[:, :] if t == 0 else e_sc[:, t - 1, 0:(t + 1) * P], recurrence)
                output(i, "out", KT // 2)

            def gla(i):
                split_units(i, "g_lr", 1)
                project(i, "q", GH)
                project(i, "k", GH)
                dve.wait_ge(gs["keep"], 2)
                for n in range(GH):
                    z = g_kr[:, n, :]
                    split_units(i, "v", 1, 2 * n)
                    dve.wait_ge(gs["ln"], n + 1)
                    if n > 0:
                        dve.wait_ge(gs["e"], 2 * n)
                    link(nc.vector.scalar_tensor_tensor(tmp[:, 1, :], z, 0.0, tmp[:, 0, :], ALU.min, ALU.subtract))
                    nc.vector.tensor_tensor_scan(tmp[:, 2, :], g_keep[:, :], tmp[:, 1, :], 0.0, ALU.mult, ALU.add)\
                        .then_inc(gs["G"], 1)
                    dve.wait_ge(gs["G"], 2 * n + 1)
                    G = tmp[:, 2, :].rearrange("p (c t) -> p c t", t=CH)
                    nc.vector.tensor_tensor(tmp[:, 3, :].rearrange("p (c t) -> p c t", t=CH),
                                            G[:, :, CH - 1:CH].to_broadcast([P, SEQ // CH, CH]), G, ALU.subtract)\
                        .then_inc(gs["G"], 1)
                    split_units(i, "v", 1, 2 * n + 1)
                    dve.wait_ge(p_free, PT0[i, "k"] + GH + 2)
                    dve.wait_ge(gs["e"], 2 * n + 2)
                    nc.vector.tensor_copy(g_dec[:, n, :],
                                          g_t[:, 0, :].rearrange("p (c t) -> p c t", t=CH)[:, :, CH - 1])
                    nc.vector.scalar_tensor_tensor(g_q[:, n, :], g_q[:, n, :], GDK ** -0.5, g_t[:, 0, :],
                                                   ALU.mult, ALU.mult).then_inc(gs["qk"], 1)
                    nc.vector.tensor_tensor(z, g_k[:, n, :], tmp[:, 3, :], ALU.mult).then_inc(gs["qk"], 1)
                    nc.vector.tensor_tensor(g_k[:, n, :], g_k[:, n, :], g_t[:, 1, :], ALU.mult).then_inc(gs["qk"], 1)
                project(i, "r", KT)
                dve.wait_ge(gs["qk"], 3 * GH)
                dve.wait_ge(gs["zero"], 1)
                dve.wait_ge(gs["mask"], 3)
                for w in range(TT * GH):
                    T, n = w // GH, w % GH
                    dve.wait_ge(gs["att_full"], w + 1)
                    if w >= 2:
                        dve.wait_ge(gs["o_full"], w - 1)
                    nc.vector.copy_predicated(g_att[:, w % 2, :], g_mask[:, :].bitcast(mybir.dt.int32),
                                              bank(w % 2)[:, 0:P]).then_inc(gs["att"], 1)
                    dve.wait_ge(gs["u_full"], w + 1)
                    for a in range(2):
                        c = 2 * T + a
                        if c == SEQ // CH - 1:
                            break
                        new, up = g_S[:, n, (c + 1) % 3, :], bank(2 + 4 * a + w % 2)[:, 0:GDV]
                        if c == 0:
                            ins = nc.vector.tensor_copy(new, up)
                        else:
                            ins = nc.vector.scalar_tensor_tensor(new, g_S[:, n, c % 3, :], g_dec[:, n, c:c + 1], up,
                                                                 ALU.mult, ALU.add)
                        link(ins) if a == 0 and c != SEQ // CH - 2 else ins.then_inc(gs["S"], 1)
                    if w % GH == GH - 1 and T > 0:
                        mean(T - 1)
                        normed(T - 1)
                mean(TT - 1)
                normed(TT - 1)
                for T in range(TT):
                    gated(i, T)
                output(i, "out", KT // 2)

            def mean(T):
                dve.wait_ge(gs["osq"], GH * (T + 1))
                inv = g_st[:, 1, GH * T:GH * (T + 1)]
                link(nc.vector.tensor_scalar(inv, g_st[:, 0, GH * T:GH * (T + 1)], 1.0 / GDV, EPS, ALU.mult, ALU.add))
                link(nc.vector.reciprocal(inv, inv))

            def normed(T):
                if T == 0:
                    dve.wait_ge(gs["gain_in"], 16)
                dve.wait_ge(gs["root"], T + 1)
                at = slice(GH * T, GH * (T + 1))
                link(nc.vector.tensor_tensor(g_st[:, 2, at], g_st[:, 1, at], g_st[:, 3, at], ALU.mult))
                for n in range(GH):
                    o = f[:, T, n * GDV:(n + 1) * GDV]
                    nc.vector.scalar_tensor_tensor(o, o, g_st[:, 2, T * GH + n:T * GH + n + 1], g_gain[:, :],
                                                   ALU.mult, ALU.mult).then_inc(gs["on"], 1)

            def gated(i, T):
                if T >= 2:
                    dve.wait_ge(gs["y_ready"], 2 * (T - 1))
                for b in range(2):
                    dve.wait_ge(gs["oT"], 2 * T + b + 1)
                    if T == 0 and b == 0:
                        dve.wait_ge(p_free, PT0[i, "r"] + KT + 2)
                    y = tmp[:, 2 * (T % 2) + b, :].rearrange("p (k c) -> p k c", k=4)
                    nc.vector.tensor_tensor(y, bank(2 * (T % 2) + b).rearrange("p (k c) -> p k c", k=4),
                                            g_r[:, 4 * b:4 * b + 4, T * P:(T + 1) * P], ALU.mult).then_inc(gs["y"], 1)
                for b in range(2):
                    dve.wait_ge(gs["y_hi"], 2 * T + b + 1)
                    y = tmp[:, 2 * (T % 2) + b, :].rearrange("p (k c) -> p k c", k=4)
                    nc.vector.tensor_tensor(x_lo[:, 4 * b:4 * b + 4, T * P:(T + 1) * P], y,
                                            x_hi[:, 4 * b:4 * b + 4, T * P:(T + 1) * P].bitcast(f32),
                                            ALU.subtract).then_inc(gs["y_ready"], 1)

            for i in range(NP + 1):
                lower = norm(i)
                if i < NP:
                    if parts[i][0] == "ffn":
                        ffn(i)
                    elif parts[i][0] == "cross":
                        cross(i, lower)
                    elif parts[i][0] == "even":
                        even(i)
                    else:
                        gla(i)

        @block.tensor
        def _(pe):
            pe.sem_inc(w_free, 2)
            pe.wait_ge(consts, 5)

            def turn_x(i, t):
                pe.wait_ge(xs_ready, TT * i + t + 1)
                if t >= 2:
                    pe.wait_ge(x_ready, 2 * TT * i + 2 * (t - 2) + 2)
                for b in range(2):
                    for k in range(4):
                        last = nc.tensor.transpose(bank(4 + 2 * (t % 2) + b)[:, k * P:(k + 1) * P],
                                                   f[:, t, (4 * b + k) * P:(4 * b + k + 1) * P], ident[:, :])
                    last.then_inc(xT_ready, 1)

            def norm(i, b0):
                u0, h0 = U[i, UNITS[parts[i][0]][0][0]], SEQ // 2

                def half_unit(q, hf):
                    u = u0 + q
                    pe.wait_ge(w_ready, u + 1)
                    return unit_blocks(u % 2, bank(b0[q])[:, hf * h0:(hf + 1) * h0], slice(hf * h0, (hf + 1) * h0))

                turn_x(i, 0)
                turn_x(i, 1)
                if i > 0:
                    pe.wait_ge(x_ready, 2 * TT * i + TT)
                    half_unit(0, 0)
                turn_x(i, 2)
                turn_x(i, 3)
                if i == 0:
                    half_unit(0, 0)
                half_unit(1, 0)
                pe.wait_ge(x_ready, 2 * TT * (i + 1))
                for q in range(2):
                    half_unit(q, 1).then_inc(w_free, 1)

            def unit_blocks(s, dst, cols_of_x):
                for b in range(UB):
                    last = three(dst, w_hi[:, s, b * P:(b + 1) * P], w_lo[:, s, b * P:(b + 1) * P],
                                 x_hi[:, b, cols_of_x], x_lo[:, b, cols_of_x], b == 0, b == UB - 1)
                return last

            def ffn(i):
                n0, u0 = nffn[i] * FT, U[i, "gate_up"]
                pe.wait_ge(gu_free, n0 + 1)
                norm(i, (0, 1))

                def pair(j, jj):
                    pe.wait_ge(gu_free, j + (n0 + 1))
                    unit_tile(pe, 2 * j + u0, u0 % 2, bank(2 * jj), x_hi, x_lo)
                    unit_tile(pe, 2 * j + (u0 + 1), (u0 + 1) % 2, bank(2 * jj + 1), x_hi, x_lo)

                pair(1, 1)
                with pe.Fori(1, FT // 2) as it:
                    pair(2 * it, 0)
                    pair(2 * it + 1, 1)
                output(i, "down", FT // 2, act_hi, act_lo)

            def output(i, seg, nu, src_hi, src_lo):
                u0, n0 = U[i, seg], nffn[i] * FT

                def half(hf, w_slot):
                    if parts[i][0] == "ffn":
                        pe.wait_ge(gu_free, hf * 2 + (n0 + FT))
                    for q in range(nu):
                        if parts[i][0] == "ffn":
                            pe.wait_ge(act_ready, n0 + 2 * q + 4)
                        pe.wait_ge(w_ready, hf * nu + (u0 + q + 1))
                        for t in range(TT):
                            dst = bank(4 - 4 * hf + t) if isinstance(hf, int) else ps[:, bass.ds(hf * -4 + (4 + t), 1), :]
                            for j in range(2):
                                wh, wl = w_slot(q, j)
                                ah, al = (a[:, 2 * q + j, t * P:(t + 1) * P] for a in (src_hi, src_lo))
                                last = streamed(dst, ah, al, wh, wl, q + j == 0, q == nu - 1 and j == 1)
                            if q == nu - 1 and t < TT - 1:
                                last.then_inc(o_full, 1)
                        last.then_inc(w_free, 1)
                        if q == 1 and mem_next and hf == 1:
                            mem_turn(i)

                def static_slot(hf):
                    return lambda q, j: [w[:, (u0 + hf * nu + q) % 2, j * SEQ:(j + 1) * SEQ] for w in (w_hi, w_lo)]

                mem_next = i + 1 < NP and parts[i + 1][0] == "cross"
                if mem_next:
                    half(0, static_slot(0))
                    half(1, static_slot(1))
                elif nu % 2 == 0:
                    with pe.Fori(0, 2) as hf:
                        half(hf, static_slot(0))
                else:
                    with pe.Fori(0, 2) as hf:
                        def slot(q, j):
                            at = bass.ds(hf * -1 + 1 if (u0 + q) % 2 else hf * 1, 1)
                            return [w[:, at, j * SEQ:(j + 1) * SEQ] for w in (w_hi, w_lo)]
                        half(hf, slot)

            def streamed(dst, ah, al, wh, wl, start, stop):
                nc.tensor.matmul(dst, ah, wh, start=start, stop=False)
                nc.tensor.matmul(dst, ah, wl, start=False, stop=False)
                return nc.tensor.matmul(dst, al, wh, start=False, stop=stop)

            def project_tile(i, seg, j, jj, xh, xl, w=SEQ):
                u0, t0 = U[i, seg], PT0[i, seg]
                pe.wait_ge(p_free, j + (t0 + 1))
                unit_tile(pe, j + u0, (u0 + jj) % 2, bank((t0 + jj) % 2)[:, 0:w], xh, xl)

            def project(i, seg, n, xh, xl, w=SEQ, done=0):
                if done % 2:
                    project_tile(i, seg, done, 1, xh, xl, w)
                with pe.Fori((done + 1) // 2, n // 2) as it:
                    for jj in range(2):
                        project_tile(i, seg, 2 * it + jj, jj, xh, xl, w)

            def values(i, seg, group, units, off, xh, xl, tiles, b0):
                for q in range(units):
                    v = U[i, seg] + off + q
                    pe.wait_ge(w_ready, v + 1)
                    for j in range(2):
                        wh, wl = (w[:, v % 2, j * SEQ:(j + 1) * SEQ] for w in (w_hi, w_lo))
                        k = 2 * q + j
                        for t in range(tiles):
                            ah, al = (a[:, k, t * P:(t + 1) * P] for a in (xh, xl))
                            dst = bank(b0 + t)
                            first, final = k == 0, k == 2 * units - 1
                            last = streamed(dst, ah, al, wh, wl, first, final)
                    last.then_inc(w_free, 1)

            def attend(i, heads, p, pT, nk, scores, mix, direct):
                a0 = A0[i]
                N = heads * TT
                for step in range(N + 4):
                    if step < N:
                        if step >= 2:
                            pe.wait_ge(at_e if direct else at_sm, a0 + step - 1)
                        scores(step // TT, step % TT, bank(step % 2)).then_inc(at_s, 1)
                    if 2 <= step < N + 2:
                        s2 = step - 2
                        pe.wait_ge(at_p, a0 + s2 + 1)
                        if s2 >= 2:
                            pe.wait_ge(at_pT, a0 + s2 - 1)
                        for k in range(nk(s2 % TT)):
                            last = nc.tensor.transpose(bank(2 + s2 % 2)[:, k * P:(k + 1) * P],
                                                       p[:, s2 % 3, k * P:(k + 1) * P], ident[:, :])
                        last.then_inc(at_t, 1)
                    if step >= 3 and (step - 3) % TT == TT - 1:
                        g = (step - 3) // TT
                        pe.wait_ge(at_pT, a0 + TT * (g + 1))
                        mix(g)

            def mem_turn(i):
                c = ncross[i + 1]
                pe.wait_ge(f_ready, TT * (2 * i + 1))
                for m in range(MT):
                    pe.wait_ge(mem_n, MT * c + m + 1)
                    for b in range(2):
                        for k in range(4):
                            last = nc.tensor.transpose(bank(4 + 2 * m + b)[:, k * P:(k + 1) * P],
                                                       c_mem[:, m, (4 * b + k) * P:(4 * b + k + 1) * P], ident[:, :])
                        last.then_inc(memT_ready, 1)

            def cross(i):
                c = ncross[i]
                pe.wait_ge(memT_used, 4 * (c + 1))
                pe.wait_ge(f_ready, TT * (2 * i - 1) + 2)
                for k in range(KT):
                    project_tile(i, "k", k, k % 2, c_mem_hi, c_mem_lo, NMEM)
                    if k in (4, 6, 7):
                        turn_x(i, {4: 0, 6: 1, 7: 2}[k])
                values(i, "v", 0, 4, 0, c_mem_hi, c_mem_lo, MT, 2)
                turn_x(i, TT - 1)
                pe.wait_ge(p_free, PT0[i, "k"] + KT + 2)
                values(i, "v", 1, 4, 4, c_mem_hi, c_mem_lo, MT, 0)
                pe.wait_ge(x_ready, 2 * TT * (i + 1))
                pe.wait_ge(v_ready, V0[i] + 2)
                project(i, "q", KT, x_hi, x_lo)
                pe.wait_ge(p_free, PT0[i, "q"] + KT + 2)
                pe.wait_ge(v_ready, V0[i] + 2)

                def scores(g, t, dst):
                    for j in range(2):
                        last = nc.tensor.matmul(dst[:, 0:NMEM], c_qT[:, 2 * g + j, t * P:(t + 1) * P],
                                                c_kT[:, 2 * g + j, :], start=j == 0, stop=j == 1)
                    return last

                def mix(g):
                    if g > 0:
                        pe.wait_ge(at_olo, O0[i] + 2 * g)
                    for o in range(2):
                        for m in range(MT):
                            last = nc.tensor.matmul(bank(4 + o), c_v[:, m, g * XD + o * P:g * XD + (o + 1) * P],
                                                    c_pT[:, g % 2, m, :], start=m == 0, stop=m == MT - 1)
                        last.then_inc(at_o, 1)

                attend(i, XH, c_p, c_pT, lambda t: MT, scores, mix, True)
                pe.wait_ge(at_olo, O0[i] + 2 * XH)
                output(i, "out", KT // 2, x_hi, x_lo)

            def one_tile(i, seg):
                pe.wait_ge(p_free, PT0[i, seg] + 1)
                u = U[i, seg]
                unit_tile(pe, u, u % 2, bank(PT0[i, seg] % 2), x_hi, x_lo)

            def even(i):
                t0 = PT0[i, "q_idx"]
                pe.wait_ge(p_free, t0 + 2)
                norm(i, (t0 % 2, 1 - t0 % 2))
                project(i, "q_idx", 4, x_hi, x_lo, done=2)
                project(i, "c_kv", 2, x_hi, x_lo)
                one_tile(i, "kw_idx")
                for k in range(2):
                    pe.wait_ge(e["sq"], k + 1)
                    last = nc.tensor.matmul(bank(4), ones[:, :], tmp[:, k, :], start=k == 0, stop=k == 1)
                last.then_inc(e["ssq"], 1)
                pe.wait_ge(p_free, PT0[i, "kw_idx"] + 3)
                for t in range(TT):
                    last = nc.tensor.transpose(bank(3)[:, t * IH:(t + 1) * IH], e_wi[:, t * P:(t + 1) * P],
                                               ident[0:IH, 0:IH])
                last.then_inc(e["wT"], 1)
                pe.wait_ge(e["w"], 1)
                for n in range((TT - 1) * IH):
                    b, hd = n // IH + 1, n % IH
                    p0 = hd % 2 * ID
                    if n >= 2:
                        pe.wait_ge(e["relu"], n - 1)
                    nc.tensor.matmul(bank(2 + n % 2)[:, 0:(b + 1) * P], e_qi[p0:p0 + ID, hd // 2, b * P:(b + 1) * P],
                                     e_k2[p0:p0 + ID, 0:(b + 1) * P], start=True, stop=True).then_inc(e["s"], 1)
                project(i, "x_b", 4, x_hi, x_lo)
                pe.wait_ge(e["ck_ready"], 2)
                u = U[i, "uk"]
                pe.wait_ge(w_ready, u + 1)
                for n in range(4):
                    pe.wait_ge(p_free, PT0[i, "uk"] + n + 1)
                    for k in range(2):
                        c = (2 * n + k) * P
                        last = three(bank((PT0[i, "uk"] + n) % 2), w_hi[:, u % 2, c:c + P], w_lo[:, u % 2, c:c + P],
                                     e_ck_hi[:, k, :], e_ck_lo[:, k, :], k == 0, k == 1)
                    last.then_inc(e["uk_full"] if n < 3 else w_free, 1)
                values(i, "uv", 0, 1, 0, e_ck_hi, e_ck_lo, TT, 4)
                project(i, "gate", 4, x_hi, x_lo)
                pe.wait_ge(e["bd"], 64)
                pe.wait_ge(v_ready, V0[i] + 1)
                pe.wait_ge(e["relu"], (TT - 1) * IH)
                for n in range(2 * LRUT):
                    pe.wait_ge(e["conv"], n % LRUT + 1)
                    if n >= 6:
                        pe.wait_ge(e["sig"], n - 5)
                    nc.tensor.matmul(bank(gate_bank[n]), e_bd[:, n // LRUT, n % LRUT, :], e_xc[:, n % LRUT, :],
                                     start=True, stop=True).then_inc(e["gates"], 1)
                project(i, "q", 4, x_hi, x_lo)
                pe.wait_ge(p_free, PT0[i, "q"] + 4 + 2)
                pe.wait_ge(e["sig"], 2 * LRUT)

                def scores(g, t, dst):
                    p0, w = g % 2 * AD, (t + 1) * P
                    return nc.tensor.matmul(dst[:, 0:w], e_qT[p0:p0 + AD, g // 2, t * P:(t + 1) * P],
                                            e_kT[p0:p0 + AD, g // 2, 0:w], start=True, stop=True)

                def mix(g):
                    p0, j = g % 2 * AD, g // 2
                    if g % 2 == 0 and j >= 2:
                        pe.wait_ge(at_olo, O0[i] + j - 1)
                    for k in range(TT):
                        last = nc.tensor.matmul(bank(4 + j % 2)[p0:p0 + AD, k * P:SEQ], e_v[:, k, g * AD:(g + 1) * AD],
                                                e_pT[:, g % 2, k, k * P:SEQ], start=k == 0, stop=k == TT - 1)
                    if g % 2:
                        last.then_inc(at_o, 1)

                attend(i, AH, e_p, e_pT, lambda t: t + 1, scores, mix, False)
                pe.wait_ge(at_olo, O0[i] + AH // 2)
                pe.wait_ge(e["y_ready"], LRUT)
                output(i, "out", KT // 2, x_hi, x_lo)

            def gla(i):
                t0 = PT0[i, "g_lr"]
                pe.wait_ge(p_free, t0 + 2)
                norm(i, (t0 % 2, 1 - t0 % 2))
                project(i, "q", GH, x_hi, x_lo, done=1)
                pe.wait_ge(gs["w2_in"], 16)
                for n in range(GH):
                    nc.tensor.matmul(bank(4 + n), g_w2[:, n * GDK:(n + 1) * GDK], g_lr[:, :], start=True, stop=True)\
                        .then_inc(gs["z_full"], 1)
                project(i, "k", GH, x_hi, x_lo)
                pe.wait_ge(gs["z"], GH)
                values(i, "v", 0, 4, 0, x_hi, x_lo, TT, 4)
                pe.wait_ge(p_free, PT0[i, "k"] + GH + 2)
                values(i, "v", 1, 4, 4, x_hi, x_lo, TT, 0)
                pe.wait_ge(v_ready, V0[i] + 1)
                for n in range(GH):
                    pe.wait_ge(gs["qk"], 3 * n + 2)
                    for t in range(TT):
                        last = nc.tensor.transpose(bank(4 + n)[:, t * P:(t + 1) * P], g_kr[:, n, t * P:(t + 1) * P],
                                                   ident[:, :])
                    last.then_inc(gs["krT"], 1)
                pe.wait_ge(v_ready, V0[i] + 2)
                project(i, "r", KT, x_hi, x_lo)
                pe.wait_ge(gs["krt"], GH)
                pe.wait_ge(p_free, PT0[i, "r"] + KT + 2)
                pe.wait_ge(gs["qk"], 3 * GH)

                def mixed(w):
                    T, n = w // GH, w % GH
                    pe.wait_ge(gs["att"], w + 1)
                    pe.wait_ge(gs["S"], w + 1)
                    if w >= 2:
                        pe.wait_ge(gs["osq"], w - 1)
                    dst = bank(4 + w % 2)
                    nc.tensor.matmul(dst[:, 0:GDV], g_att[:, w % 2, :], g_v[:, T, n * GDV:(n + 1) * GDV],
                                     start=True, stop=False, skip_group_check=True)
                    for a in range(2):
                        c = 2 * T + a
                        if c == 0:
                            continue
                        last = nc.tensor.matmul(dst[a * CH:(a + 1) * CH, 0:GDV], g_q[:, n, c * CH:(c + 1) * CH],
                                                g_S[:, n, c % 3, :], start=False, stop=a == 1, skip_group_check=True)
                    last.then_inc(gs["o_full"], 1)

                for w in range(TT * GH + 1):
                    if w < TT * GH:
                        T, n = w // GH, w % GH
                        if w >= 2:
                            pe.wait_ge(gs["att"], w - 1)
                        nc.tensor.matmul(bank(w % 2)[:, 0:P], g_k[:, n, T * P:(T + 1) * P], g_q[:, n, T * P:(T + 1) * P],
                                         start=True, stop=True).then_inc(gs["att_full"], 1)
                        if w >= 2:
                            pe.wait_ge(gs["S"], w - 1)
                        for a in range(2):
                            rows = slice(a * CH, (a + 1) * CH)
                            last = nc.tensor.matmul(bank(2 + 4 * a + w % 2)[:, 0:GDV], g_krt[rows, T, n, :],
                                                    g_v[rows, T, n * GDV:(n + 1) * GDV], start=True, stop=True)
                        last.then_inc(gs["u_full"], 1)
                    if w >= 1:
                        mixed(w - 1)
                for T in range(TT):
                    pe.wait_ge(gs["on"], GH * (T + 1))
                    if T >= 2:
                        pe.wait_ge(gs["y"], 2 * (T - 1))
                    for b in range(2):
                        for k in range(4):
                            last = nc.tensor.transpose(bank(2 * (T % 2) + b)[:, k * P:(k + 1) * P],
                                                       f[:, T, (4 * b + k) * P:(4 * b + k + 1) * P], ident[:, :])
                        last.then_inc(gs["oT"], 1)
                pe.wait_ge(gs["y_ready"], 2 * TT)
                output(i, "out", KT // 2, x_hi, x_lo)

            for i in range(NP):
                if parts[i][0] == "ffn":
                    ffn(i)
                elif parts[i][0] == "cross":
                    cross(i)
                elif parts[i][0] == "even":
                    even(i)
                else:
                    gla(i)


def square_units(w):
    K, N = w.shape
    kb = -(-K // UW) * UB
    padded = np.zeros((kb * P, N), w.dtype)
    padded[:K] = w
    return padded.reshape(kb // UB, UB, P, N // P, P).transpose(3, 0, 2, 1, 4).reshape(-1, P, UW)


def padded_columns(w, n):
    out = np.zeros((w.shape[0], n), w.dtype)
    out[:, :w.shape[1]] = w
    return out


def row_units(w):
    K, N = w.shape
    return w.reshape(K // (2 * P), 2, P, N // 512, 512).transpose(3, 0, 2, 1, 4).reshape(-1, P, UW)


def weight_stream(a, parts):
    units = []
    for kind, l, k in parts:
        if kind == "ffn":
            gu = square_units(a["ffn_w_gu"][l, k])
            units.append(gu.reshape(2, FT, P, UW).transpose(1, 0, 2, 3).reshape(-1, P, UW))
            units.append(row_units(a["ffn_w_down"][l, k]))
        elif kind == "cross":
            kv = a["xa_w_kv"][l]
            units += [square_units(kv[:, :DM]), row_units(kv[:, DM:]), square_units(a["xa_w_q"][l]),
                      row_units(a["xa_w_o"][l])]
        elif kind == "even":
            e = l // 2
            w = a["ev_w_in"][e]
            q, ckv, qi, ki, wi, gate, xb = np.split(w, np.cumsum([512, RANK, IH * ID, ID, IH, 512]), axis=1)
            units += [square_units(qi), square_units(ckv),
                      square_units(padded_columns(np.concatenate([ki, wi], 1), P)), square_units(xb)]
            uk = a["ev_w_uk"][e].reshape(2, P, 4, P).transpose(1, 2, 0, 3).reshape(1, P, UW)
            units += [uk, row_units(a["ev_w_uv"][e]), square_units(gate), square_units(q),
                      row_units(a["ev_w_out"][e])]
        else:
            o = l // 2
            q, k_, v, g, r = np.split(a["od_w_in"][o], np.cumsum([512, 512, DM, GR]), axis=1)
            units += [square_units(padded_columns(g, P)), square_units(q), square_units(k_), row_units(v),
                      square_units(r), row_units(a["od_w_out"][o])]
    return np.ascontiguousarray(np.concatenate(units))


def arrays_for(a, parts):
    a = {k: np.asarray(v) for k, v in a.items()}
    norms = a["norms"]
    pre = {"ffn": (0, 7), "even": (2, 2), "gla": (2, 2), "cross": (4, 4)}
    post = {"ffn": (1, 8), "even": (3, 3), "gla": (3, 3), "cross": (5, 5)}

    def column(v):
        return v.reshape(-1, P).T

    cols = [column(a["ev_kv_norm"][0])]
    cols += [a["ev_conv_w"][0].reshape(CONV, LRUT, P).transpose(2, 1, 0).reshape(P, -1)]
    cols += [column(a[n][0]) for n in ("ev_conv_b", "ev_b_ra", "ev_b_ri", "ev_lam", "od_b_g")]
    return {
        "x": a["x"][0], "mem": a["mem"][0], "wstream": weight_stream(a, parts),
        "cols": np.ascontiguousarray(np.concatenate(cols, 1)),
        "gains": np.stack([norms[l, pre[kind][k]] for kind, l, k in parts]),
        "post_gains": np.stack([norms[l, post[kind][k]] for kind, l, k in parts]),
        "mem_gains": np.ascontiguousarray(norms[:, 6]),
        "head_gain": a["od_head_norm"][:1],
        "w_ra": a["ev_w_ra"][0], "w_ri": a["ev_w_ri"][0], "w_g2": a["od_w_g2"][0],
    }


def kernel(**inputs):
    import concourse.bacc as _bacc
    from concourse.bass_utils import run_bass_kernel_spmd as _run

    nc = _bacc.Bacc("TRN2", target_bir_lowering=False, num_devices=1)
    arrays = {f"in_{k}": np.ascontiguousarray(v) for k, v in arrays_for(inputs, PARTS).items()}
    args = [nc.dram_tensor(k, v.shape, mybir.dt.from_np(v.dtype), kind="ExternalInput").ap() for k, v in arrays.items()]
    out = nc.dram_tensor("out_0_dram", (SEQ, DM), mybir.dt.float32, kind="ExternalOutput").ap()
    trunk(nc, PARTS, *args, out)
    r = _run(nc, [arrays], core_ids=[0])
    return r.results[0]["out_0_dram"].reshape(1, SEQ, DM)
```
